# Optimizing a Trainium2 kernel written in Bass

```python
import math
import jax
import jax.numpy as jnp
from jax import lax
import numpy as np

D_MODEL = 1024
BATCH = 1
SEQ = 256
DEPTH = 2

CTX_LEN = 256
GRID_W = 64
N_MOD = 9
D_FF = 2816
RMS_EPS = 1e-6

HG_HEADS = 4
HG_DK = 128
HG_DV = 128
HG_K = HG_HEADS * HG_DK
HG_V = HG_HEADS * HG_DV
HG_CHUNK = 64

HY_W = 512
HY_ORDER = 2
HY_EMB = 33
HY_BANDS = (HY_EMB - 1) // 2
HY_FH = 64
HY_TARGET = 1e-2
HY_MIN_DECAY = math.log(HY_TARGET) / 1.5
HY_MAX_DECAY = math.log(HY_TARGET) / 0.3
HY_SHIFT = 0.05

MLA_HEADS = 4
MLA_Q_LORA = 256
MLA_KV_LORA = 128
MLA_NOPE = 128
MLA_ROPE = 64
MLA_V = 128
MLA_QK = MLA_NOPE + MLA_ROPE
MLA_OUT = MLA_HEADS * MLA_V
MLA_SCALE = MLA_QK ** -0.5
ROPE_THETA = 10000.0
Q_BLOCK = 128

IN_SPLITS = (HG_K, HG_K, HG_K, HG_V, HG_V, 3 * HY_W, MLA_Q_LORA, MLA_KV_LORA, MLA_ROPE, D_MODEL, D_MODEL, D_MODEL)
IN_COLS = sum(IN_SPLITS)

kernel_name = 'hybrid_hgrn2_hyena_mla_dit_block'

def rmsnorm(x, g):
    xf = x.astype(jnp.float32)
    y = xf * lax.rsqrt(jnp.mean(xf * xf, axis=-1, keepdims=True) + RMS_EPS)
    return (y * g.astype(jnp.float32)).astype(x.dtype)

def adaln(x, g, shift, scale):
    return rmsnorm(x, g) * (1 + scale) + shift

def swiglu(h, w13, w2):
    a, b = jnp.split(h @ w13, 2, axis=-1)
    return (jax.nn.silu(a) * b) @ w2

def short_conv3(u, w, b):
    up = jnp.pad(u, ((0, 0), (1, 1), (0, 0)))
    return up[:, :-2] * w[0] + up[:, 1:-1] * w[1] + up[:, 2:] * w[2] + b

def gla_scan(q, k, v, logf, s0):
    bsz, t_len, n_h, dk = q.shape
    nc = t_len // HG_CHUNK

    def to_chunks(a):
        a = a.astype(jnp.float32).reshape(bsz, nc, HG_CHUNK, n_h, a.shape[-1])
        return jnp.moveaxis(a, (1, 3), (0, 2))

    tri = jnp.tril(jnp.ones((HG_CHUNK, HG_CHUNK), bool))[:, :, None]

    def step(state, inp):
        qc, kc, vc, gc = inp
        b = jnp.cumsum(gc, axis=2)
        b_last = b[:, :, -1:, :]
        o_inter = jnp.einsum('bhtk,bhkv->bhtv', qc * jnp.exp(b), state)
        diff = b[:, :, :, None, :] - b[:, :, None, :, :]
        decay = jnp.where(tri, jnp.exp(jnp.where(tri, diff, 0.0)), 0.0)
        attn = jnp.einsum('bhtsk,bhsk->bhts', decay * qc[:, :, :, None, :], kc)
        o = o_inter + jnp.einsum('bhts,bhsv->bhtv', attn, vc)
        new_state = jnp.exp(b_last[:, :, 0, :])[..., None] * state + jnp.einsum(
            'bhsk,bhsv->bhkv', kc * jnp.exp(b_last - b), vc)
        return new_state, o

    s_final, o = lax.scan(step, s0.astype(jnp.float32), (to_chunks(q), to_chunks(k), to_chunks(v), to_chunks(logf)))
    o = jnp.moveaxis(o, (0, 2), (1, 3)).reshape(bsz, t_len, n_h, v.shape[-1])
    return o, s_final

def split_heads(a, d):
    return a.reshape(a.shape[0], a.shape[1], -1, d)

def hgrn2_gates(z, lb):
    f = lb + (1.0 - lb) * jax.nn.sigmoid(z.astype(jnp.float32))
    return 1.0 - f, jnp.log(f)

def hgrn2_seq(q, i, zf, zb, lb_f, lb_b, s0f, s0b):
    qh = split_heads(jax.nn.silu(q), HG_DK) * HG_DK ** -0.5
    ih = split_heads(i, HG_DV)
    kf, lf = hgrn2_gates(split_heads(zf, HG_DK), lb_f.reshape(HG_HEADS, HG_DK))
    kb, lbk = hgrn2_gates(split_heads(zb, HG_DK), lb_b.reshape(HG_HEADS, HG_DK))
    o_f, s_f = gla_scan(qh, kf, ih, lf, s0f)
    flip = lambda a: jnp.flip(a, axis=1)
    o_b, s_b = gla_scan(flip(qh), flip(kb), flip(ih), flip(lbk), s0b)
    return o_f + flip(o_b), s_f, s_b

def hgrn2_readout(o, g, gain):
    o = rmsnorm(o, gain)
    return o.reshape(o.shape[0], o.shape[1], HG_V).astype(g.dtype) * jax.nn.silu(g)

def hyena_filters(L, p):
    f32 = jnp.float32
    t = jnp.linspace(0.0, 1.0, L, dtype=f32)[:, None]
    w = (2.0 * math.pi / L) * jnp.arange(L, dtype=f32)[:, None]
    bands = jnp.linspace(1e-4, HY_BANDS - 1, HY_BANDS, dtype=f32)[None, :]
    emb = jnp.concatenate([t, jnp.cos(bands * w), -jnp.sin(bands * w)], axis=-1)
    freq = p['hy_freq'].astype(f32)
    hid = jnp.sin(freq * (emb @ p['hy_w1'].astype(f32) + p['hy_b1'].astype(f32)))
    hid = jnp.sin(freq * (hid @ p['hy_w2'].astype(f32) + p['hy_b2'].astype(f32)))
    hid = jnp.sin(freq * (hid @ p['hy_w3'].astype(f32) + p['hy_b3'].astype(f32)))
    h = (hid @ p['hy_w4'].astype(f32)).reshape(L, 2, HY_ORDER, HY_W)
    deltas = jnp.abs(jnp.linspace(HY_MIN_DECAY, HY_MAX_DECAY, HY_W, dtype=f32))
    h = h * (jnp.exp(-t[:, :, None, None] * deltas) + HY_SHIFT)
    h_fwd = h[:, 0]
    h_bwd = h[1:, 1]
    norm = jnp.sum(jnp.abs(h_fwd), axis=0) + jnp.sum(jnp.abs(h_bwd), axis=0)
    k_circ = jnp.concatenate([h_fwd, jnp.zeros((1, HY_ORDER, HY_W), f32), h_bwd[::-1]], axis=0) / norm
    return jnp.fft.rfft(k_circ, axis=0)

def fft_conv(u, kf):
    L = u.shape[1]
    U = jnp.fft.rfft(u.astype(jnp.float32), n=2 * L, axis=1)
    return jnp.fft.irfft(U * kf[None], n=2 * L, axis=1)[:, :L].astype(u.dtype)

def hyena(u3, p, kf):
    uc = short_conv3(u3, p['hy_conv_w'], p['hy_conv_b'])
    x1, x2, z = jnp.split(uc, 3, axis=-1)
    for o, xg in enumerate((x1, x2)):
        z = xg * (fft_conv(z, kf[:, o]) + z * p['hy_skip'][o])
    return z

def axial_angles(L):
    rows = L // GRID_W
    row = jnp.repeat(jnp.arange(rows, dtype=jnp.float32), GRID_W)
    col = jnp.tile(jnp.arange(GRID_W, dtype=jnp.float32), rows)
    half = MLA_ROPE // 2
    inv = ROPE_THETA ** (-jnp.arange(0, half, 2, dtype=jnp.float32) / half)
    return row[:, None] * inv, col[:, None] * inv

def rotate(x, ang):
    x1, x2 = jnp.split(x, 2, axis=-1)
    cos = jnp.cos(ang).astype(x.dtype)
    sin = jnp.sin(ang).astype(x.dtype)
    return jnp.concatenate([x1 * cos - x2 * sin, x2 * cos + x1 * sin], axis=-1)

def axial_rope(x, ang_r, ang_c):
    xr, xc = jnp.split(x, 2, axis=-1)
    return jnp.concatenate([rotate(xr, ang_r), rotate(xc, ang_c)], axis=-1)

def mla_queries(qa, p):
    bsz, L, _ = qa.shape
    q = (rmsnorm(qa, p['q_a_norm']) @ p['w_uq']).reshape(bsz, L, MLA_HEADS, MLA_QK)
    return rmsnorm(q[..., :MLA_NOPE], p['q_nope_norm']), rmsnorm(q[..., MLA_NOPE:], p['q_rope_norm'])

def mla_keys(kva, kr, p):
    bsz, L, _ = kva.shape
    kv = (rmsnorm(kva, p['kv_a_norm']) @ p['w_ukv']).reshape(bsz, L, MLA_HEADS, MLA_NOPE + MLA_V)
    return rmsnorm(kv[..., :MLA_NOPE], p['k_nope_norm']), rmsnorm(kr, p['k_rope_norm']), kv[..., MLA_NOPE:]

def mla_attend(qn, qr, key_sets):
    s = jnp.concatenate([jnp.einsum('bqhd,bkhd->bhqk', qn, kn) + jnp.einsum('bqhr,bkr->bhqk', qr, kr)
                         for kn, kr, _ in key_sets], axis=-1)
    pr = jax.nn.softmax(s.astype(jnp.float32) * MLA_SCALE, axis=-1)
    out = 0.0
    start = 0
    for _, _, v in key_sets:
        n = v.shape[1]
        out = out + jnp.einsum('bhqk,bkhd->bqhd', pr[..., start:start + n].astype(v.dtype), v)
        start += n
    return out

def latent_attention(qn, qr, kn, kr, v, kn_c, kr_c, v_c):
    bsz, L = qn.shape[0], qn.shape[1]
    nb = L // Q_BLOCK
    blocks = lambda a: jnp.moveaxis(a.reshape(bsz, nb, Q_BLOCK, *a.shape[2:]), 1, 0)
    out = lax.map(lambda qb: mla_attend(qb[0], qb[1], ((kn, kr, v), (kn_c, kr_c, v_c))), (blocks(qn), blocks(qr)))
    return jnp.moveaxis(out, 0, 1).reshape(bsz, L, MLA_OUT)

def merge(y_a, y_b, y_c, g_a, g_b, g_c, p):
    m = (jax.nn.sigmoid(g_a) * (y_a @ p['w_br_a']) + jax.nn.sigmoid(g_b) * (y_b @ p['w_br_b'])
         + jax.nn.sigmoid(g_c) * (y_c @ p['w_br_c']))
    return m @ p['w_out']

def token_mixer(h, hc, p, lb_f, lb_b, need_ctx):
    offs = np.cumsum(IN_SPLITS)[:-1].tolist()
    (q, zf, zb, iv, g, hy, qa, kva, kr, ga, gb, gc) = jnp.split(h @ p['w_in'], offs, axis=-1)
    (q_c, zf_c, zb_c, iv_c, g_c, hy_c, qa_c, kva_c, kr_c, ga_c, gb_c, gc_c) = jnp.split(hc @ p['w_in'], offs, axis=-1)
    bsz, L = h.shape[0], h.shape[1]
    Lc = hc.shape[1]

    zero = jnp.zeros((bsz, HG_HEADS, HG_DK, HG_DV), jnp.float32)
    o_ctx, s_f, s_b = hgrn2_seq(q_c, iv_c, zf_c, zb_c, lb_f, lb_b, zero, zero)
    o_lat, _, _ = hgrn2_seq(q, iv, zf, zb, lb_f, lb_b, s_f, s_b)
    y_a = hgrn2_readout(o_lat, g, p['hg_out_norm'])

    y_b = hyena(hy, p, hyena_filters(L, p))

    ang_r, ang_c = axial_angles(L)
    qn, qr = mla_queries(qa, p)
    qr = axial_rope(qr, ang_r[:, None], ang_c[:, None])
    kn, krr, v = mla_keys(kva, kr, p)
    krr = axial_rope(krr, ang_r, ang_c)
    kn_c, krr_c, v_c = mla_keys(kva_c, kr_c, p)
    y_c = latent_attention(qn, qr, kn, krr, v, kn_c, krr_c, v_c)

    out = merge(y_a, y_b, y_c, ga, gb, gc, p)
    if not need_ctx:
        return out, None
    y_a_c = hgrn2_readout(o_ctx, g_c, p['hg_out_norm'])
    y_b_c = hyena(hy_c, p, hyena_filters(Lc, p))
    qn_c, qr_c = mla_queries(qa_c, p)
    y_c_c = mla_attend(qn_c, qr_c, ((kn_c, krr_c, v_c),)).reshape(bsz, Lc, MLA_OUT)
    out_c = merge(y_a_c, y_b_c, y_c_c, ga_c, gb_c, gc_c, p)
    return out, out_c

def half_ffn(y, m, idx, norm, w13, w2):
    return y + 0.5 * m[idx + 2] * swiglu(adaln(y, norm, m[idx], m[idx + 1]), w13, w2)

def layer(x, xc, c, c_ctx, p, lb_f, lb_b, need_ctx):
    mod = jnp.split((jax.nn.silu(c) @ p['ada_w'] + p['ada_b'])[:, None, :], N_MOD, axis=-1)
    mod_c = jnp.split((jax.nn.silu(c_ctx) @ p['ada_w'] + p['ada_b'])[None, None, :], N_MOD, axis=-1)
    x = half_ffn(x, mod, 0, p['ffn1_norm'], p['ffn1_w13'], p['ffn1_w2'])
    xc = half_ffn(xc, mod_c, 0, p['ffn1_norm'], p['ffn1_w13'], p['ffn1_w2'])
    out, out_c = token_mixer(adaln(x, p['mix_norm'], mod[3], mod[4]),
                             adaln(xc, p['mix_norm'], mod_c[3], mod_c[4]), p, lb_f, lb_b, need_ctx)
    x = x + mod[5] * out
    x = half_ffn(x, mod, 6, p['ffn2_norm'], p['ffn2_w13'], p['ffn2_w2'])
    if need_ctx:
        xc = xc + mod_c[5] * out_c
        xc = half_ffn(xc, mod_c, 6, p['ffn2_norm'], p['ffn2_w13'], p['ffn2_w2'])
    return x, xc

def setup_inputs(seed: int = 0) -> dict:
    key = jax.random.key(seed)
    keys = iter(jax.random.split(key, 64))

    def normal(shape, scale=1.0):
        return scale * jax.random.normal(next(keys), shape, jnp.float32)

    def gain(shape):
        return 1.0 + normal(shape, 0.02)

    L, D = DEPTH, D_MODEL
    return {
        'x': normal((BATCH, SEQ, D)),
        'c': normal((BATCH, D)),
        'ctx': normal((BATCH, CTX_LEN, D)),
        'c_ctx': normal((D,)),
        'ada_w': normal((L, D, N_MOD * D), 0.5 * D ** -0.5),
        'ada_b': normal((L, N_MOD * D), 0.02),
        'ffn1_norm': gain((L, D)),
        'ffn1_w13': normal((L, D, 2 * D_FF), D ** -0.5),
        'ffn1_w2': normal((L, D_FF, D), D_FF ** -0.5),
        'mix_norm': gain((L, D)),
        'w_in': normal((L, D, IN_COLS), D ** -0.5),
        'hg_lb_logits': normal((2, L, HG_K), 0.5),
        'hg_out_norm': gain((L, HG_DV)),
        'hy_conv_w': normal((L, 3, 3 * HY_W), 3 ** -0.5),
        'hy_conv_b': normal((L, 3 * HY_W), 0.02),
        'hy_w1': normal((L, HY_EMB, HY_FH), HY_EMB ** -0.5),
        'hy_b1': normal((L, HY_FH), 0.1),
        'hy_w2': normal((L, HY_FH, HY_FH), HY_FH ** -0.5),
        'hy_b2': normal((L, HY_FH), 0.1),
        'hy_w3': normal((L, HY_FH, HY_FH), HY_FH ** -0.5),
        'hy_b3': normal((L, HY_FH), 0.1),
        'hy_w4': normal((L, HY_FH, 2 * HY_ORDER * HY_W), HY_FH ** -0.5),
        'hy_freq': gain((L, HY_FH)),
        'hy_skip': normal((L, HY_ORDER, HY_W), 0.5),
        'q_a_norm': gain((L, MLA_Q_LORA)),
        'w_uq': normal((L, MLA_Q_LORA, MLA_HEADS * MLA_QK), MLA_Q_LORA ** -0.5),
        'kv_a_norm': gain((L, MLA_KV_LORA)),
        'w_ukv': normal((L, MLA_KV_LORA, MLA_HEADS * (MLA_NOPE + MLA_V)), MLA_KV_LORA ** -0.5),
        'q_nope_norm': gain((L, MLA_NOPE)),
        'q_rope_norm': gain((L, MLA_ROPE)),
        'k_nope_norm': gain((L, MLA_NOPE)),
        'k_rope_norm': gain((L, MLA_ROPE)),
        'w_br_a': normal((L, HG_V, D), HG_V ** -0.5),
        'w_br_b': normal((L, HY_W, D), HY_W ** -0.5),
        'w_br_c': normal((L, MLA_OUT, D), MLA_OUT ** -0.5),
        'w_out': normal((L, D, D), D ** -0.5),
        'ffn2_norm': gain((L, D)),
        'ffn2_w13': normal((L, D, 2 * D_FF), D ** -0.5),
        'ffn2_w2': normal((L, D_FF, D), D_FF ** -0.5),
    }

def reference(x, c, ctx, c_ctx, ada_w, ada_b, ffn1_norm, ffn1_w13, ffn1_w2, mix_norm, w_in,
              hg_lb_logits, hg_out_norm, hy_conv_w, hy_conv_b, hy_w1, hy_b1, hy_w2, hy_b2, hy_w3, hy_b3,
              hy_w4, hy_freq, hy_skip, q_a_norm, w_uq, kv_a_norm, w_ukv, q_nope_norm, q_rope_norm,
              k_nope_norm, k_rope_norm, w_br_a, w_br_b, w_br_c, w_out, ffn2_norm, ffn2_w13, ffn2_w2):
    stacked = {
        'ada_w': ada_w, 'ada_b': ada_b, 'ffn1_norm': ffn1_norm, 'ffn1_w13': ffn1_w13, 'ffn1_w2': ffn1_w2,
        'mix_norm': mix_norm, 'w_in': w_in, 'hg_out_norm': hg_out_norm,
        'hy_conv_w': hy_conv_w, 'hy_conv_b': hy_conv_b, 'hy_w1': hy_w1, 'hy_b1': hy_b1, 'hy_w2': hy_w2,
        'hy_b2': hy_b2, 'hy_w3': hy_w3, 'hy_b3': hy_b3, 'hy_w4': hy_w4, 'hy_freq': hy_freq, 'hy_skip': hy_skip,
        'q_a_norm': q_a_norm, 'w_uq': w_uq, 'kv_a_norm': kv_a_norm, 'w_ukv': w_ukv,
        'q_nope_norm': q_nope_norm, 'q_rope_norm': q_rope_norm, 'k_nope_norm': k_nope_norm,
        'k_rope_norm': k_rope_norm, 'w_br_a': w_br_a, 'w_br_b': w_br_b, 'w_br_c': w_br_c, 'w_out': w_out,
        'ffn2_norm': ffn2_norm, 'ffn2_w13': ffn2_w13, 'ffn2_w2': ffn2_w2,
    }
    lbs = jax.nn.softmax(hg_lb_logits.astype(jnp.float32), axis=1)
    lbs = jnp.cumsum(lbs, axis=1) - lbs[:, :1]
    xc = ctx
    for l in range(DEPTH):
        p = {name: val[l] for name, val in stacked.items()}
        x, xc = layer(x, xc, c, c_ctx, p, lbs[0, l], lbs[1, l], l < DEPTH - 1)
    return x


_drawn_inputs = setup_inputs


def setup_inputs(seed=0):
    import zlib

    import numpy as np

    out = dict(_drawn_inputs(seed))
    spreads = {}
    factors = {'ctx': 4.477,
     'ffn1_norm': 8.0,
     'mix_norm': 8.0,
     'hg_lb_logits': 8.0,
     'hg_out_norm': 41.209,
     'hy_conv_b': 8.0,
     'hy_b1': 8.0,
     'hy_b2': 8.0,
     'hy_b3': 8.0,
     'hy_freq': 8.0,
     'q_a_norm': 34.178,
     'kv_a_norm': 45.058,
     'q_nope_norm': 41.571,
     'q_rope_norm': 58.846,
     'k_nope_norm': 38.324,
     'k_rope_norm': 53.125,
     'ffn2_norm': 41.386}
    for name, (base, spread) in spreads.items():
        noise = np.random.default_rng([zlib.crc32(name.encode()), seed]).standard_normal(out[name].shape)
        drawn = base * np.exp(spread * noise) if base else spread * noise
        out[name] = jnp.asarray(drawn.astype(out[name].dtype))
    for name, factor in factors.items():
        out[name] = (out[name] * factor).astype(out[name].dtype)
    return out
```

```python
import math
from contextlib import ExitStack

import concourse.bass as bass
import numpy as np
from concourse import mybir

P = 128
D, T, S, L = 1024, 512, 256, 2
DT = D // P
FF = 2816
FT = FF // P
NMOD = 9
H = 4
DK = 128
CH = T // P
QK = 192
ROPE = 64
EPS = 1e-6
HYW, FH, EMB = 512, 64, 33
CT = HYW // P
LEVELS = [0, 64, 32, 16, 8, 4, 2, 1]
SCALE = QK ** -0.5
TINY = 2.0 ** -62
TWO_PI = 2.0 * math.pi
PI_A, PI_B = 6.28125, 0.00193500518798828125
PI_C = TWO_PI - PI_A - PI_B
ROUND = 1.5 * 2.0 ** 23
UP_CHUNK, DOWN_CHUNK, PROJ_CHUNK, ADA_CHUNK = 8 * 256, FT * P, 8 * 256, 8 * 512
KVKR_CHUNK, MLA_CHUNK, MERGE_CHUNK = 8 * 192, 2 * 768 + 1024, 8 * 256 + 4 * 256
SLOT = max(UP_CHUNK, DOWN_CHUNK, MERGE_CHUNK, MLA_CHUNK)
ADA_CHUNKS = NMOD * D // 512
ADA_SLOTS = 6

SMALL = {}
_at = 0
for _name, _n in (("ffn1_norm", 8), ("mix_norm", 8), ("ffn2_norm", 8), ("ada_b", 72), ("hg_out_norm", 1),
                  ("conv_w", 36), ("conv_b", 12), ("b1", 1), ("b2", 1), ("b3", 1), ("freq", 1), ("skip", 8),
                  ("q_a_norm", 2), ("kv_a_norm", 1), ("q_nope_norm", 1), ("q_rope_norm", 1),
                  ("k_nope_norm", 1), ("k_rope_norm", 1), ("w1", FH), ("w2", FH), ("w3", FH)):
    SMALL[_name] = (_at, _n)
    _at += _n
NSMALL = _at
FIXED = {"ident": (0, 128), "cos": (128, 256), "sin": (384, 256), "perm": (640, 64), "emb": (704, 256)}
NFIXED = 960


class Signal:

    def __init__(self, sem, keys):
        self.sem, self.value, self.made = sem, {k: i + 1 for i, k in enumerate(keys)}, 0

    def wait(self, eng, key):
        eng.wait_ge(self.sem, self.value[key])

    def of(self, key):
        self.made += 1
        assert self.value[key] == self.made, (key, self.made)
        return self.sem, self.made


class Steps:

    def __init__(self, eng, sem):
        self.eng, self.sem, self.n, self.last = eng, sem, 0, None

    def __call__(self, ins, event=None):
        if event is None:
            self.n += 1
            event = (self.sem, self.n)
        ins.then_inc(event[0], 1)
        self.last = event

    def settle(self):
        if self.last:
            self.eng.wait_ge(*self.last)


def build(nc, dram, out):
    F32 = mybir.dt.float32
    ACT, ALU, AX = mybir.ActivationFunctionType, mybir.AluOpType, mybir.AxisListType
    with ExitStack() as ctx:
        def sb(name, shape, dt=F32):
            return ctx.enter_context(nc.sbuf_tensor(name, shape, dt))

        def sem(name):
            return ctx.enter_context(nc.semaphore(name))

        xT = sb("xT", [P, DT, T])
        hT = sb("hT", [P, DT, T])
        ring = sb("ring", [P, 2, SLOT])
        fixed = sb("fixed", [P, NFIXED])
        masks = sb("masks", [P, len(LEVELS), P], mybir.dt.int32)
        small = sb("small", [P, L, NSMALL])
        cT = sb("cT", [P, DT, 2])
        mod = sb("mod", [P, L, 72, 2])
        gain_s = sb("gain_s", [P, L, 3, DT, 2])
        gate_s = sb("gate_s", [P, L, 3, DT, 2])
        logits = sb("logits", [P, 2, L, H])
        lb_e = sb("lb_e", [P, 2, L, H])
        lb_t = sb("lb_t", [P, 2, 2, H])
        lb = sb("lb", [P, 2, L, H])
        lb1 = sb("lb1", [P, 2, L, H])
        ones = {n: sb(f"ones{n}", [P, P]) for n in (1, 1024, 256, 128, 64)}
        eps_t = sb("eps_t", [P, 1])
        root = sb("root", [P, T])
        rnorm = sb("rnorm", [P, 8])
        elast = sb("elast", [P, 2, 16])
        mxt = sb("mxt", [P, 4, 4])
        R = sb("R", [P, 16 * 2048 + 1040])

        def unit(u, shape, off=0, p=P):
            n = int(np.prod(shape))
            a = R[0:p, u * 2048 + off:u * 2048 + off + n]
            if len(shape) == 2:
                return a.rearrange("p (a b) -> p a b", b=shape[1])
            if len(shape) == 3:
                return a.rearrange("p (a b c) -> p a b c", b=shape[1], c=shape[2])
            if len(shape) == 4:
                return a.rearrange("p (a b c d) -> p a b c d", b=shape[1], c=shape[2], d=shape[3])
            return a

        ada_w = [unit(2 * s, (8, 512)) for s in range(ADA_SLOTS)]
        g_ff = unit(0, (FT, T))
        silu_ff = unit(6, (2, T))
        q = unit(0, (H, T))
        kd = [unit(1, (H, T)), unit(2, (H, T))]
        bd = [unit(3, (H, T)), unit(4, (H, T))]
        attn = unit(5, (H, CH, P))
        split = unit(6, (2, H, T))
        lev = [unit(6 + i, (2, 2, T)) for i in range(3)]
        val = unit(9, (CH, HYW))
        ya = unit(10, (H, T))
        tail = [unit(6, (H, T)), unit(7, (H, T))]
        kdT = [unit(6, (3, 512)), unit(7, (3, 512))]
        state = [unit(8, (3, 512)), unit(15, (3, 512))]
        o_raw, o_sq, o_root = unit(1, (H, T)), unit(2, (H, T)), unit(0, (H, T))
        uc = unit(11, (3 * CT, T))
        upad = unit(16, (2, 2, S + 2))
        spectrum = unit(0, (2, 2, 2, HYW))
        hy_tab = unit(2, (4096,))
        dft = hy_tab[:, 0:2048].rearrange("p (m t f) -> p m t f", m=4, t=2)
        window = hy_tab[:, 2048:4096].rearrange("p (w t c) -> p w t c", w=2, t=2)
        w4 = unit(4, (4 * HYW,), p=FH)
        taps = unit(5, (2, 4, HYW))
        even_odd = unit(7, (2, 2, 2, HYW))
        zt = unit(9, (CH, HYW))
        arg = unit(15, (S,), 0, FH)
        turns = unit(15, (S,), 256, FH)
        hid = unit(15, (S,), 512, FH)
        prod = unit(15, (4, HYW))
        spec_y = [unit(5, (2, 2, HYW)), unit(6, (2, 2, HYW))]
        yb = unit(13, (CT, T))
        raw = unit(14, (4, T))
        qn, qr, kn = unit(0, (H, T)), unit(1, (H, T), 0, ROPE), unit(2, (H, T))
        kr = unit(3, (T,), 0, ROPE)
        rope_t = unit(3, (S,), 512, ROPE)
        vv = unit(4, (CH, 512))
        lora = unit(5, (3, T))
        m_sq, m_root, m_raw = unit(6, (4, T)), unit(7, (4, T)), unit(9, (4, T))
        prob = unit(12, (4, T))
        probT = unit(8, (2, CH, P))
        yc = unit(11, (H, T))
        mix = unit(0, (DT, T))
        gate_t = unit(2, (2, T))
        part_t = unit(3, (2, T))

        ps = [ctx.enter_context(nc.psum_tensor(f"ps{i}", [P, 512], F32)) for i in range(8)]

        ident = fixed[:, 0:128]
        cosT, sinT = fixed[0:ROPE, 128:384], fixed[0:ROPE, 384:640]
        perm, emb = fixed[0:ROPE, 640:704], fixed[0:EMB, 704:960]

        def sm(l, name, j=0, n=1, p=P):
            at = SMALL[name][0] + j
            return small[0:p, l, at:at + n]

        ps_full = [sem(f"ps_full{i}") for i in range(8)]
        ps_free = [sem(f"ps_free{i}") for i in range(8)]
        landed = [sem("weights0"), sem("weights1")]
        ada_landed = [sem(f"ada{i}") for i in range(ADA_SLOTS)]
        params_in, x_in, hy_in, y_out = sem("params_in"), sem("x_in"), sem("hy_in"), sem("y_out")
        LW = [(l, w) for l in range(L) for w in range(3)]
        widths = {(l, w): (T if l < L - 1 or w < 2 else S) for l, w in LW}
        out_w = [T if l < L - 1 else S for l in range(L)]

        def signal(name, keys):
            return Signal(sem(name), list(keys))
        c_silu = signal("c_silu", [0])
        consts = signal("consts", [0])
        coef = signal("coef", [0])
        lb_max = signal("lb_max", [0])
        lb_exp = signal("lb_exp", [0])
        squared = signal("squared", [(l, w, d) for l, w in LW for d in range(DT)])
        scaled = signal("scaled", [(l, w, d) for l, w in LW for d in range(DT)])
        h_ready = signal("h_ready", [(l, w, d) for l, w in LW for d in range(DT)])
        f_split = signal("f_split", [(l, n) for l in range(L) for n in range(8)])
        logged = signal("logged", [(l, n) for l in range(L) for n in range(8)])
        conv_done = signal("conv_done", [(l, j) for l in range(L) for j in range(12)])
        NLEV = 2 * len(LEVELS)
        LN = [(l, n) for l in range(L) for n in range(NLEV)]
        diffs = signal("diffs", LN)
        decays = signal("decays", [(l, n) for l, n in LN if n % len(LEVELS)])
        weighted = signal("weighted", [(l, n) for l, n in LN if n % len(LEVELS)])
        LDIR = [(l, d) for l in range(L) for d in range(2)]
        tail_diff = signal("tail_diff", LDIR)
        tail_exp = signal("tail_exp", LDIR)
        k_decayed = signal("k_decayed", LDIR)
        q_decayed = signal("q_decayed", LDIR)
        ya_done = signal("ya_done", [(l, h) for l in range(L) for h in range(H)])
        phase = signal("phase", [(l, i) for l in range(L) for i in range(3)])
        hidden = signal("hidden", [(l, i) for l in range(L) for i in range(3)])
        taps_ready = signal("taps_ready", range(L))
        taps_abs = signal("taps_abs", range(L))
        LO = [(l, o) for l in range(L) for o in range(2)]
        spect = signal("spect", [(l, o, st, f) for l, o in LO for st in range(out_w[l] // S) for f in range(2)])
        z_done = signal("z_done", [(l, o, c) for l, o in LO for c in range(CT)])
        BATCH = [(l, b, j) for l in range(L) for b in range(4) for j in range(3 if b == 0 else 4)]
        m_squared = signal("m_squared", BATCH)
        m_normed = signal("m_normed", BATCH)
        roped = signal("roped", [(l, i) for l in range(L) for i in range(5)])
        tiles = {l: [(qt, h) for qt in range(out_w[l] // P) for h in range(H)] for l in range(L)}
        SC = [(l, i) for l in range(L) for i in range(len(tiles[l]))]
        row_max = signal("row_max", SC)
        exped = signal("exped", SC)
        prob_ready = signal("prob_ready", SC)
        mixed = signal("mixed", [(l, d) for l in range(L) for d in range(DT)])
        vector_steps, scalar_steps = sem("vector_steps"), sem("scalar_steps")

        chunk_at, order = {}, []
        for l in range(L):
            for key, n in (("up0", 22), ("down0", 8), ("proj", 17), ("kvkr", 1), ("mla", 1), ("merge", 12),
                           ("out", 4), ("up1", 22), ("down1", 8)):
                chunk_at[l, key] = len(order)
                order += [(l, key, j) for j in range(n)]
        released = {}
        use = {}
        bank_uses = [0] * 8
        rr = [0]

        block = ctx.enter_context(nc.Block())

        @block.tensor
        def _(pe):
            mm = nc.tensor.matmul

            def bank(key, b=None):
                if b is None:
                    b = rr[0] % 8
                    rr[0] += 1
                if bank_uses[b]:
                    pe.wait_ge(ps_free[b], bank_uses[b])
                bank_uses[b] += 1
                use[key] = (b, bank_uses[b])
                return b

            def taken(key):
                b, n = use[key]
                pe.wait_ge(ps_free[b], n)

            def weights(c):
                pe.wait_ge(landed[c % 2], 16 * (c // 2 + 1))
                return ring[:, c % 2, :]

            def used(c, key):
                released[c] = use[key]

            def ada():
                c_silu.wait(pe, 0)
                with pe.Fori(0, L * ADA_CHUNKS // ADA_SLOTS) as i:
                    for s in range(ADA_SLOTS):
                        pe.wait_ge(ada_landed[s], i * 16 + 16)
                        if s < 2:
                            pe.wait_ge(ps_free[s], i * 3 + bank_uses[s])
                        else:
                            pe.wait_ge(ps_free[s % 2], i * 3 + bank_uses[s % 2] + s // 2)
                        for j in range(4):
                            for k in range(DT):
                                last = mm(ps[s % 2][:, 2 * j:2 * j + 2], ada_w[s][:, k, j * P:(j + 1) * P],
                                          cT[:, k, :], start=k == 0, stop=k == DT - 1)
                        last.then_inc(ps_full[s % 2], 1)
                for b in range(2):
                    use["ada", b] = (b, bank_uses[b] + 1)
                    bank_uses[b] += 3 * L * ADA_CHUNKS // ADA_SLOTS

            def warm():
                consts.wait(pe, 0)
                for b in range(8):
                    mm(ps[b][:, 0:P], ones[1][:, :], ones[1][:, :], start=True, stop=True).then_inc(ps_full[b], 1)
                    bank_uses[b] += 1

            def norm(l, w):
                W = widths[l, w]
                b = bank(("stat", l, w))
                for d in range(DT):
                    squared.wait(pe, (l, w, d))
                    last = mm(ps[b][:, 0:W], ones[1024][:, :], hT[:, d, 0:W], start=d == 0, stop=d == DT - 1)
                last.then_inc(ps_full[b], 1)

            def ffn(l, f):
                w = 2 * f
                W = widths[l, w]
                c0 = chunk_at[l, f"up{f}"]
                h_ready.wait(pe, (l, w, DT - 1))
                base = list(bank_uses)
                with pe.Fori(0, FT // 2) as i:
                    for s in range(2):
                        c = c0 + s
                        pe.wait_ge(landed[c % 2], i * 16 + 16 * (c // 2 + 1))
                        wt = ring[:, c % 2, 0:UP_CHUNK].rearrange("p (ab k n) -> p ab k n", ab=2, k=DT)
                        for ab in range(2):
                            b = 2 * s + ab
                            pe.wait_ge(ps_free[b], i + base[b])
                            for k in range(DT):
                                last = mm(ps[b][:, 0:W], wt[:, ab, k, :], hT[:, k, 0:W], start=k == 0, stop=k == DT - 1)
                            last.then_inc(ps_full[b], 1)
                for b in range(4):
                    use["up", l, f, b] = (b, base[b] + 1)
                    bank_uses[b] += FT // 2
                for c in range(c0, c0 + FT):
                    released[c] = (2 * ((c - c0) % 2) + 1, base[2 * ((c - c0) % 2) + 1] + 1 + (c - c0) // 2)
                for b in (1, 3):
                    pe.wait_ge(ps_free[b], bank_uses[b])
                c0 = chunk_at[l, f"down{f}"]
                base = list(bank_uses)
                with pe.Fori(0, DT // 2) as i:
                    for s in range(2):
                        c = c0 + s
                        pe.wait_ge(landed[c % 2], i * 16 + 16 * (c // 2 + 1))
                        wt = ring[:, c % 2, 0:DOWN_CHUNK].rearrange("p (k n) -> p k n", n=P)
                        b = 4 + s
                        pe.wait_ge(ps_free[b], i + base[b])
                        for k in range(FT):
                            last = mm(ps[b][:, 0:W], wt[:, k, :], g_ff[:, k, 0:W], start=k == 0, stop=k == FT - 1)
                        last.then_inc(ps_full[b], 1)
                for d in range(DT):
                    use["down", l, f, d] = (4 + d % 2, base[4 + d % 2] + 1 + d // 2)
                    released[c0 + d] = use["down", l, f, d]
                for b in (4, 5):
                    bank_uses[b] += DT // 2

            def project(l, c, kind, j, W):
                wt = weights(c)[:, 0:PROJ_CHUNK].rearrange("p (k n) -> p k n", k=DT)
                b = bank((kind, l, j))
                for k in range(DT):
                    last = mm(ps[b][:, 0:W], wt[:, k, (j % 2) * P:(j % 2 + 1) * P], hT[:, k, 0:W],
                              start=k == 0, stop=k == DT - 1)
                last.then_inc(ps_full[b], 1)
                used(c, (kind, l, j))

            def level(l, n):
                pair, li = n // len(LEVELS), n % len(LEVELS)
                buf = lev[n % 3]
                (weighted if li else diffs).wait(pe, (l, n))
                for hh in range(2):
                    b = bank(("lev", l, n, hh))
                    for c in range(out_w[l] // P):
                        cols = slice(c * P, (c + 1) * P)
                        rhs = q[:, 2 * pair + hh, cols] if li == 0 else buf[:, 0, hh, cols]
                        last = mm(ps[b][:, cols], buf[:, 1, hh, cols], rhs, start=True, stop=True)
                    last.then_inc(ps_full[b], 1)

            def mixer_in(l):
                W = out_w[l]
                c = chunk_at[l, "proj"]
                h_ready.wait(pe, (l, 1, DT - 1))
                for kind, width in (("zf", T), ("zb", T), ("q", W)):
                    for j in range(4):
                        project(l, c + j // 2, kind, j, width)
                    c += 2
                for half in range(2):
                    wt = weights(c)[:, 0:PROJ_CHUNK].rearrange("p (k n) -> p k n", k=DT)
                    for t in range(CH):
                        b = bank(("v", l, half, t))
                        for k in range(DT):
                            last = mm(ps[b][:, 0:256], hT[:, k, t * P:(t + 1) * P], wt[:, k, :],
                                      start=k == 0, stop=k == DT - 1)
                        last.then_inc(ps_full[b], 1)
                    used(c, ("v", l, half, CH - 1))
                    c += 1
                for j in range(4):
                    project(l, c + j // 2, "g", j, W)
                c += 2
                for n in range(NLEV):
                    if n < 12:
                        project(l, c + n // 2, "hy", n, W)
                    elif n < 14:
                        project(l, c + 6, "qa", n - 12, W)
                    else:
                        kc = chunk_at[l, "kvkr"]
                        wt = weights(kc)[:, 0:KVKR_CHUNK].rearrange("p (k n) -> p k n", k=DT)
                        lo, m = ((0, P), (P, ROPE))[n - 14]
                        b = bank(("kvkr", l, n - 14))
                        for k in range(DT):
                            last = mm(ps[b][0:m, 0:T], wt[:, k, lo:lo + m], hT[:, k, 0:T], start=k == 0, stop=k == DT - 1)
                        last.then_inc(ps_full[b], 1)
                        used(kc, ("kvkr", l, n - 14))
                    level(l, n)

            def hgrn_out(l):
                W = out_w[l]
                seq = ((2, 3, 0), (3, 2, 1))
                for dr in range(2):
                    k_decayed.wait(pe, (l, dr))
                    for j, c in enumerate(seq[dr]):
                        b = bank(("kT", l, dr, j))
                        for h in range(H):
                            last = nc.tensor.transpose(ps[b][:, h * P:(h + 1) * P], kd[dr][:, h, c * P:(c + 1) * P], ident)
                        last.then_inc(ps_full[b], 1)
                for j in range(3):
                    for dr in range(2):
                        taken(("kT", l, dr, j))
                        c = seq[dr][j]
                        b = bank(("st", l, j, dr))
                        for h in range(H):
                            cols = slice(h * P, (h + 1) * P)
                            last = mm(ps[b][:, cols], kdT[dr][:, j, cols], val[:, c, cols], start=True, stop=True)
                        last.then_inc(ps_full[b], 1)
                q_decayed.wait(pe, (l, 1))
                taken(("st", l, 2, 1))
                before = ({3: 0, 0: 1, 1: 2}, {2: 0, 1: 1, 0: 2})
                for h in range(H):
                    b = bank(("o", l, h))
                    hc = slice(h * P, (h + 1) * P)
                    for c in range(W // P):
                        cols = slice(c * P, (c + 1) * P)
                        terms = [(val[:, c, hc], attn[:, h, c, :])]
                        for dr in range(2):
                            if c in before[dr]:
                                terms.append((state[dr][:, before[dr][c], hc], bd[dr][:, h, cols]))
                        for i, (a, r) in enumerate(terms):
                            last = mm(ps[b][:, cols], a, r, start=i == 0, stop=i == len(terms) - 1)
                    last.then_inc(ps_full[b], 1)
                for h in range(H):
                    taken(("o", l, h))
                    b = bank(("ostat", l, h))
                    mm(ps[b][:, 0:W], ones[128][:, :], o_sq[:, h, 0:W], start=True, stop=True).then_inc(ps_full[b], 1)

            def hyena(l):
                W = out_w[l]
                for i, name in enumerate(("w1", "w2", "w3")):
                    b = bank(("mlp", l, i))
                    if i:
                        hidden.wait(pe, (l, i - 1))
                    else:
                        pe.wait_ge(hy_in, 32 * (l + 1))
                    k = EMB if i == 0 else FH
                    mm(ps[b][0:FH, 0:S], sm(l, name, 0, FH, k), emb if i == 0 else hid, start=True, stop=True)\
                        .then_inc(ps_full[b], 1)
                hidden.wait(pe, (l, 2))
                for t in range(2):
                    for cc in range(4):
                        b = bank(("tap", l, t, cc))
                        mm(ps[b][:, :], hid[:, t * P:(t + 1) * P], w4[:, cc * HYW:(cc + 1) * HYW],
                           start=True, stop=True).then_inc(ps_full[b], 1)
                taps_ready.wait(pe, l)
                for o in range(2):
                    for f in range(2):
                        for part in range(2):
                            b = bank(("kf", l, o, f, part))
                            for t in range(2):
                                last = mm(ps[b][:, :], dft[:, part, t, f * P:(f + 1) * P], even_odd[:, part, t, o, :],
                                          start=t == 0, stop=t == 1)
                            last.then_inc(ps_full[b], 1)
                taps_abs.wait(pe, l)
                b = bank(("l1", l))
                for o in range(2):
                    for ct in range(CT):
                        for i in range(4):
                            t, dr = i // 2, i % 2
                            col = o * CT + ct
                            last = mm(ps[b][:, col:col + 1], taps[:, t, 2 * dr + o, ct * P:(ct + 1) * P], ones[1][:, 0:1],
                                      start=i == 0, stop=i == 3)
                last.then_inc(ps_full[b], 1)
                for o in range(2):
                    if o:
                        z_done.wait(pe, (l, 0, CT - 1))
                    else:
                        conv_done.wait(pe, (l, 11))
                    for t in range(W // P):
                        b = bank(("zt", l, o, t))
                        for ct in range(CT):
                            last = nc.tensor.transpose(ps[b][:, ct * P:(ct + 1) * P], yb[:, ct, t * P:(t + 1) * P], ident)
                        last.then_inc(ps_full[b], 1)
                    for st in range(W // S):
                        taken(("zt", l, o, 2 * st + 1))
                        for f in range(2):
                            for part in range(2):
                                b = bank(("fw", l, o, st, f, part))
                                for t in range(2):
                                    last = mm(ps[b][:, :], dft[:, part, t, f * P:(f + 1) * P], zt[:, 2 * st + t, :],
                                              start=t == 0, stop=t == 1)
                                last.then_inc(ps_full[b], 1)
                    spect.wait(pe, (l, o, W // S - 1, 1))
                    for ct in range(CT):
                        b = bank(("inv", l, o, ct))
                        for st in range(W // S):
                            for i in range(4):
                                f, part = i // 2, i % 2
                                last = mm(ps[b][:, st * S:(st + 1) * S], spec_y[st][:, f, part, ct * P:(ct + 1) * P],
                                          dft[:, 2 + part, f, :], start=i == 0, stop=i == 3)
                        last.then_inc(ps_full[b], 1)

            def mla(l):
                W = out_w[l]
                for j, (n_t, key) in enumerate(((2, 256), (1, 128), (1, 64))):
                    m_squared.wait(pe, (l, 0, j))
                    b = bank(("ms", l, 0, j))
                    width, p = (W, P) if j == 0 else (T, P if j == 1 else ROPE)
                    for i in range(n_t):
                        src = m_sq[0:p, (0, 2, 3)[j] + i, 0:width]
                        last = mm(ps[b][0:p, 0:width], ones[key][0:p, 0:p], src, start=i == 0, stop=i == n_t - 1)
                    last.then_inc(ps_full[b], 1)
                mc = chunk_at[l, "mla"]
                wt = weights(mc)
                uq = wt[:, 0:1536].rearrange("p (k n) -> p k n", k=2)
                ukv = wt[:, 1536:2560].rearrange("p (h n) -> p h n", h=H)
                m_normed.wait(pe, (l, 0, 1))
                for t in range(CH):
                    b = bank(("vv", l, t))
                    mm(ps[b][:, :].rearrange("p (h n) -> p h n", h=H), lora[:, 2, t * P:(t + 1) * P], ukv[:, :, P:2 * P],
                       start=True, stop=True).then_inc(ps_full[b], 1)
                for bt in range(1, 4):
                    p = ROPE if bt == 2 else P
                    width = T if bt == 3 else W
                    for h in range(H):
                        b = bank(("mp", l, bt, h))
                        if bt == 3:
                            last = mm(ps[b][:, 0:T], ukv[:, h, 0:P], lora[:, 2, :], start=True, stop=True)
                        else:
                            lo = h * QK + (P if bt == 2 else 0)
                            for k in range(2):
                                last = mm(ps[b][0:p, 0:W], uq[:, k, lo:lo + p], lora[:, k, 0:W], start=k == 0, stop=k == 1)
                        last.then_inc(ps_full[b], 1)
                    for h in range(H):
                        m_squared.wait(pe, (l, bt, h))
                        b = bank(("ms", l, bt, h))
                        mm(ps[b][0:p, 0:width], ones[64 if bt == 2 else 128][0:p, 0:p], m_sq[0:p, h, 0:width],
                           start=True, stop=True).then_inc(ps_full[b], 1)
                used(mc, ("mp", l, 3, H - 1))
                for i in range(5):
                    m_normed.wait(pe, (l, 2, i) if i < 4 else (l, 0, 2))
                    b = bank(("rope", l, i))
                    src = qr[:, i, 0:S] if i < 4 else kr[:, 0:S]
                    mm(ps[b][0:ROPE, 0:S], perm, src, start=True, stop=True).then_inc(ps_full[b], 1)
                m_normed.wait(pe, (l, 3, H - 1))
                roped.wait(pe, (l, 4))
                taken(("vv", l, CH - 1))
                n = len(tiles[l])
                for i in range(n + 2):
                    if i < n:
                        qt, h = tiles[l][i]
                        k0 = 0 if qt < 2 else S
                        b = bank(("sc", l, i))
                        cols = slice(qt * P, (qt + 1) * P)
                        mm(ps[b][:, 0:T - k0], qn[:, h, cols], kn[:, h, k0:T], start=True, stop=False)
                        mm(ps[b][:, 0:T - k0], qr[:, h, cols], kr[:, k0:T], start=False, stop=True).then_inc(ps_full[b], 1)
                    if 1 <= i <= n:
                        qt, h = tiles[l][i - 1]
                        nk = CH if qt < 2 else 2
                        prob_ready.wait(pe, (l, i - 1))
                        b = bank(("pt", l, i - 1))
                        for kt in range(nk):
                            last = nc.tensor.transpose(ps[b][:, kt * P:(kt + 1) * P],
                                                       prob[:, (i - 1) % 4, kt * P:(kt + 1) * P], ident)
                        last.then_inc(ps_full[b], 1)
                    if i >= 2:
                        qt, h = tiles[l][i - 2]
                        nk = CH if qt < 2 else 2
                        taken(("pt", l, i - 2))
                        b = bank(("av", l, i - 2))
                        for kt in range(nk):
                            last = mm(ps[b][:, 0:P], vv[:, CH - nk + kt, h * P:(h + 1) * P], probT[:, i % 2, kt, :],
                                      start=kt == 0, stop=kt == nk - 1)
                        last.then_inc(ps_full[b], 1)
                taken(("av", l, n - 1))

            def merge(l):
                W = out_w[l]
                ya_done.wait(pe, (l, H - 1))
                z_done.wait(pe, (l, 1, CT - 1))
                for br, y in enumerate((ya, yb, yc)):
                    for qd in range(4):
                        c = chunk_at[l, "merge"] + 4 * br + qd
                        wt = weights(c)
                        wg = wt[:, 0:2048].rearrange("p (k n) -> p k n", k=DT)
                        wb = wt[:, 2048:3072].rearrange("p (k n) -> p k n", k=4)
                        for dd in range(2):
                            d = 2 * qd + dd
                            cols = slice(dd * P, (dd + 1) * P)
                            b = bank(("gate", l, br, d))
                            for k in range(DT):
                                last = mm(ps[b][:, 0:W], wg[:, k, cols], hT[:, k, 0:W], start=k == 0, stop=k == DT - 1)
                            last.then_inc(ps_full[b], 1)
                            b = bank(("br", l, br, d))
                            for k in range(4):
                                last = mm(ps[b][:, 0:W], wb[:, k, cols], y[:, k, 0:W], start=k == 0, stop=k == 3)
                            last.then_inc(ps_full[b], 1)
                        used(c, ("br", l, br, 2 * qd + 1))
                mixed.wait(pe, (l, DT - 1))
                for d in range(DT):
                    c = chunk_at[l, "out"] + d // 2
                    wt = weights(c)[:, 0:PROJ_CHUNK].rearrange("p (k n) -> p k n", k=DT)
                    b = bank(("out", l, d))
                    for k in range(DT):
                        last = mm(ps[b][:, 0:W], wt[:, k, (d % 2) * P:(d % 2 + 1) * P], mix[:, k, 0:W],
                                  start=k == 0, stop=k == DT - 1)
                    last.then_inc(ps_full[b], 1)
                    used(c, ("out", l, d))

            warm()
            ada()
            for l in range(L):
                norm(l, 0)
                ffn(l, 0)
                norm(l, 1)
                mixer_in(l)
                hgrn_out(l)
                hyena(l)
                mla(l)
                merge(l)
                norm(l, 2)
                ffn(l, 1)

        def full(eng, key):
            b, n = use[key]
            eng.wait_ge(ps_full[b], n)
            return ps[b]

        def freed(key):
            b, n = use[key]
            return ps_free[b], n

        def x_ready(l, w):
            if w == 0:
                return [(x_in, 32)] * DT if l == 0 else [freed(("down", l - 1, 1, d)) for d in range(DT)]
            return [freed(("down", l, 0, d) if w == 1 else ("out", l, d)) for d in range(DT)]

        @block.sync
        def _(sp):
            sp.dma_start(cT[:, :, :], dram["cT"]).then_inc(params_in, 16)
            sp.dma_start(small[:, :, :], dram["small"]).then_inc(params_in, 16)
            sp.dma_start(logits[:, :, :, :], dram["logits"]).then_inc(params_in, 16)
            for s in range(ADA_SLOTS):
                sp.dma_start(ada_w[s], dram["ada"][s, :, :, :]).then_inc(ada_landed[s], 16)
            sp.dma_start(fixed[:, :], dram["fixed"]).then_inc(params_in, 16)
            sp.dma_start(masks[:, :, :], dram["masks"]).then_inc(params_in, 16)
            for c in range(2):
                sp.dma_start(xT[:, 4 * c:4 * c + 4, :], dram["xT"][:, 4 * c:4 * c + 4, :]).then_inc(x_in, 16)
            with sp.Fori(1, L * ADA_CHUNKS // ADA_SLOTS) as i:
                for s in range(ADA_SLOTS):
                    n = use["ada", s % 2][1]
                    sp.wait_ge(ps_full[s % 2], i * 3 + (n - 3 + s // 2))
                    sp.dma_start(ada_w[s].unsqueeze(1), dram["ada"][bass.ds(i * ADA_SLOTS + s, 1), :, :, :]
                                 .rearrange("o p k n -> p o k n")).then_inc(ada_landed[s], 16)
            source = {"proj": "proj", "kvkr": "kvkr", "mla": "mla", "merge": "merge", "out": "wout",
                      "up0": "up0", "up1": "up1", "down0": "down0", "down1": "down1"}

            def load(c):
                l, key, j = order[c]
                src = dram[source[key]][l, j, :, :]
                if c >= 2:
                    b, n = released[c - 2]
                    sp.wait_ge(ps_full[b], n)
                sp.dma_start(ring[:, c % 2, 0:src.shape[1]], src).then_inc(landed[c % 2], 16)

            def load_loop(c0, n):
                l, key, _ = order[c0]
                load(c0)
                load(c0 + 1)
                with sp.Fori(1, n // 2) as i:
                    for s in range(2):
                        b, m = released[c0 + s]
                        sp.wait_ge(ps_full[b], i + (m - 1))
                        src = dram[source[key]][l, bass.ds(i * 2 + s, 1), :, :].rearrange("o p n -> p (o n)")
                        sp.dma_start(ring[:, (c0 + s) % 2, 0:src.shape[1]], src).then_inc(landed[(c0 + s) % 2], 16)

            for l in range(L):
                for f in range(2):
                    load_loop(chunk_at[l, f"up{f}"], FT)
                    load_loop(chunk_at[l, f"down{f}"], DT)
                    if f == 1:
                        continue
                    for c in range(chunk_at[l, "proj"], chunk_at[l, "mla"]):
                        load(c)
                    full(sp, ("ostat", l, H - 1))
                    sp.dma_start(hy_tab[:, :], dram["hy_tab"]).then_inc(hy_in, 16)
                    sp.dma_start(w4, dram["w4"][l, :, :]).then_inc(hy_in, 16)
                    for c in range(chunk_at[l, "mla"], chunk_at[l, "up1"]):
                        load(c)
            for d in range(DT):
                sp.wait_ge(*freed(("down", L - 1, 1, d)))
                sp.dma_start(out[:, d, :], xT[:, d, 0:S]).then_inc(y_out, 16)
            sp.wait_ge(y_out, 16 * DT)

        @block.scalar
        def _(act):
            do = Steps(act, scalar_steps)
            A = nc.scalar.activation

            def norm(l, w):
                W = widths[l, w]
                ready = x_ready(l, w)
                for d in range(DT):
                    act.wait_ge(*ready[d])
                    do(A(hT[:, d, 0:W], xT[:, d, 0:W], ACT.Square), squared.of((l, w, d)))
                src = full(act, ("stat", l, w))
                do(A(root[:, 0:W], src[:, 0:W], ACT.Sqrt, bias=eps_t[:, :]), freed(("stat", l, w)))
                for d in range(DT):
                    scaled.wait(act, (l, w, d))
                    for st in range(W // S):
                        cols = slice(st * S, (st + 1) * S)
                        ins = A(hT[:, d, cols], hT[:, d, cols], ACT.Identity, scale=gain_s[:, l, w, d, st:st + 1],
                                bias=mod[:, l, 3 * w * DT + d, st:st + 1])
                        do(ins, h_ready.of((l, w, d)) if st == W // S - 1 else None)

            def ffn(l, f):
                W = widths[l, 2 * f]
                with act.Fori(0, FT // 2) as i:
                    for s in range(2):
                        na, nb = use["up", l, f, 2 * s][1], use["up", l, f, 2 * s + 1][1]
                        act.wait_ge(ps_full[2 * s], i + na)
                        act.wait_ge(ps_free[2 * s + 1], i + (nb - 1))
                        A(silu_ff[:, s, 0:W], ps[2 * s][:, 0:W], ACT.Silu).then_inc(ps_free[2 * s], 1)

            def take(key, dst, src_cols, func=ACT.Copy, p=P):
                src = full(act, key)
                do(A(dst, src[0:p, 0:src_cols], func), freed(key))

            def mixer_in(l):
                W = out_w[l]
                for dr, kind in enumerate(("zf", "zb")):
                    for j in range(4):
                        take((kind, l, j), kd[dr][:, j, :], T, ACT.Sigmoid)
                for j in range(4):
                    take(("q", l, j), q[:, j, 0:W], W, ACT.Silu)
                for half in range(2):
                    for t in range(CH):
                        take(("v", l, half, t), val[:, t, half * 256:(half + 1) * 256], 256)
                for n in range(8):
                    f_split.wait(act, (l, n))
                    do(A(bd[n // 4][:, n % 4, :], bd[n // 4][:, n % 4, :], ACT.Ln))
                    do(A(split[:, n // 4, n % 4, :], split[:, n // 4, n % 4, :], ACT.Ln), logged.of((l, n)))
                for j in range(4):
                    take(("g", l, j), ya[:, j, 0:W], W, ACT.Silu)
                for n in range(NLEV):
                    if n % len(LEVELS):
                        diffs.wait(act, (l, n))
                        do(A(lev[n % 3][:, :, :, 0:W], lev[n % 3][:, :, :, 0:W], ACT.Exp), decays.of((l, n)))
                    if n < 12:
                        src = full(act, ("hy", l, n))
                        if n >= 2:
                            conv_done.wait(act, (l, n - 2))
                        elif l:
                            conv_done.wait(act, (l - 1, 10 + n))
                        for st in range(W // S):
                            do(A(upad[:, n % 2, st, 1:S + 1], src[:, st * S:(st + 1) * S], ACT.Copy))
                        do(A(uc[:, n, 0:W], src[:, 0:W], ACT.Identity, scale=sm(l, "conv_w", 12 + n),
                             bias=sm(l, "conv_b", n)), freed(("hy", l, n)))
                    elif n < 14:
                        take(("qa", l, n - 12), raw[:, n - 12, 0:W], W)
                    else:
                        p = P if n == 14 else ROPE
                        take(("kvkr", l, n - 14), raw[0:p, n - 12, :], T, p=p)

            def hgrn_out(l):
                W = out_w[l]
                for dr in range(2):
                    tail_diff.wait(act, (l, dr))
                    do(A(tail[dr], tail[dr], ACT.Exp))
                    do(A(bd[dr], bd[dr], ACT.Exp), tail_exp.of((l, dr)))
                for dr in range(2):
                    for j in range(3):
                        take(("kT", l, dr, j), kdT[dr][:, j, :], 512)
                for h in range(H):
                    src = full(act, ("o", l, h))
                    do(A(o_raw[:, h, 0:W], src[:, 0:W], ACT.Copy))
                    do(A(o_sq[:, h, 0:W], src[:, 0:W], ACT.Square), freed(("o", l, h)))
                for h in range(H):
                    src = full(act, ("ostat", l, h))
                    do(A(o_root[:, h, 0:W], src[:, 0:W], ACT.Sqrt, bias=eps_t[:, :]), freed(("ostat", l, h)))

            def hyena(l):
                W = out_w[l]
                for i in range(3):
                    phase.wait(act, (l, i))
                    do(A(hid, arg, ACT.Sin), hidden.of((l, i)))
                taps_ready.wait(act, l)
                do(A(taps, taps, ACT.Abs), taps_abs.of(l))
                for o in range(2):
                    for f in range(2):
                        for part in range(2):
                            take(("kf", l, o, f, part), spectrum[:, o, f, part, :], HYW)
                for o in range(2):
                    for t in range(W // P):
                        take(("zt", l, o, t), zt[:, t, :], HYW)

            def mla(l):
                W = out_w[l]
                z_done.wait(act, (l, 1, CT - 1))
                for j, (at, n, width, p) in enumerate(((0, 2, W, P), (2, 1, T, P), (3, 1, T, ROPE))):
                    for i in range(n):
                        ins = A(m_sq[0:p, at + i, 0:width], raw[0:p, at + i, 0:width], ACT.Square)
                        do(ins, m_squared.of((l, 0, j)) if i == n - 1 else None)
                for j, (width, p) in enumerate(((W, P), (T, P), (T, ROPE))):
                    src = full(act, ("ms", l, 0, j))
                    do(A(m_root[0:p, j, 0:width], src[0:p, 0:width], ACT.Sqrt, bias=eps_t[0:p, :]), freed(("ms", l, 0, j)))
                for t in range(CH):
                    take(("vv", l, t), vv[:, t, :], 512)
                for bt in range(1, 4):
                    p = ROPE if bt == 2 else P
                    width = T if bt == 3 else W
                    for h in range(H):
                        src = full(act, ("mp", l, bt, h))
                        if bt > 1:
                            m_normed.wait(act, (l, bt - 1, h))
                        elif h == 0:
                            m_normed.wait(act, (l, 0, 2))
                        do(A(m_sq[0:p, h, 0:width], src[0:p, 0:width], ACT.Square), m_squared.of((l, bt, h)))
                        do(A(m_raw[0:p, h, 0:width], src[0:p, 0:width], ACT.Copy), freed(("mp", l, bt, h)))
                    for h in range(H):
                        src = full(act, ("ms", l, bt, h))
                        do(A(m_root[0:p, h, 0:width], src[0:p, 0:width], ACT.Sqrt, bias=eps_t[0:p, :]),
                           freed(("ms", l, bt, h)))
                n = len(tiles[l])
                for i in range(n + 2):
                    if i < n:
                        qt, h = tiles[l][i]
                        nk = T if qt < 2 else S
                        src = full(act, ("sc", l, i))
                        row_max.wait(act, (l, i))
                        if i >= 4:
                            full(act, ("pt", l, i - 4))
                        do(A(prob[:, i % 4, 0:nk], src[:, 0:nk], ACT.Exp, bias=mxt[:, i % 4, 1:2], scale=SCALE,
                             accum_out=mxt[:, i % 4, 2:3]), exped.of((l, i)))
                    if 1 <= i <= n:
                        qt, h = tiles[l][i - 1]
                        nk = T if qt < 2 else S
                        if i >= 3:
                            full(act, ("av", l, i - 3))
                        take(("pt", l, i - 1), probT[:, (i - 1) % 2, 0:nk // P, :].rearrange("p k q -> p (k q)"), nk)
                    if i >= 2:
                        qt, h = tiles[l][i - 2]
                        take(("av", l, i - 2), yc[:, h, qt * P:(qt + 1) * P], P)

            def merge(l):
                W = out_w[l]
                for br in range(3):
                    for d in range(DT):
                        n = br * DT + d
                        if n >= 2:
                            act.wait_ge(*freed(("br", l, (n - 2) // DT, (n - 2) % DT)))
                        take(("gate", l, br, d), gate_t[:, n % 2, 0:W], W, ACT.Sigmoid)

            act.wait_ge(params_in, 16 * 5)
            do(A(cT[:, :, :], cT[:, :, :], ACT.Silu), c_silu.of(0))
            consts.wait(act, 0)
            lb_max.wait(act, 0)
            do(A(lb_e[:, :, :, :], lb_e[:, :, :, :], ACT.Exp), lb_exp.of(0))
            coef.wait(act, 0)
            for l in range(L):
                norm(l, 0)
                ffn(l, 0)
                norm(l, 1)
                mixer_in(l)
                hgrn_out(l)
                hyena(l)
                mla(l)
                merge(l)
                norm(l, 2)
                ffn(l, 1)

        @block.vector
        def _(dve):
            do = Steps(dve, vector_steps)
            tt, ts, stt = nc.vector.tensor_tensor, nc.vector.tensor_scalar, nc.vector.scalar_tensor_tensor

            def then(ins, event=None):
                do(ins, event)
                do.settle()

            def setup():
                for n, t in ones.items():
                    do(nc.vector.memset(t[:, :], 1.0 / n))
                do(nc.vector.memset(upad, 0.0))
                do(nc.vector.memset(eps_t[:, :], EPS), consts.of(0))
                for b in range(8):
                    dve.wait_ge(ps_full[b], 1)
                    do(nc.vector.tensor_copy(elast[:, 0, 0:1], ps[b][:, 0:1]), (ps_free[b], 1))
                    do.settle()
                dve.wait_ge(params_in, 16 * 5)
                for l in range(L):
                    then(tt(lb_t[:, :, 0, :], logits[:, :, 0, :], logits[:, :, 1, :], ALU.max))
                for l in range(L):
                    do(tt(lb_e[:, :, l, :], logits[:, :, l, :], lb_t[:, :, 0, :], ALU.subtract),
                       lb_max.of(0) if l == L - 1 else None)
                lb_exp.wait(dve, 0)
                then(tt(lb_t[:, :, 0, :], lb_e[:, :, 0, :], lb_e[:, :, 1, :], ALU.add))
                then(nc.vector.reciprocal(lb_t[:, :, 1, :], lb_t[:, :, 0, :]))
                for l in range(L):
                    then(tt(lb_e[:, :, l, :], lb_e[:, :, l, :], lb_t[:, :, 1, :], ALU.mult))
                then(nc.vector.tensor_copy(lb_t[:, :, 0, :], lb_e[:, :, 0, :]))
                for l in range(L):
                    if l:
                        then(tt(lb_t[:, :, 0, :], lb_t[:, :, 0, :], lb_e[:, :, l, :], ALU.add))
                    then(tt(lb[:, :, l, :], lb_t[:, :, 0, :], lb_e[:, :, 0, :], ALU.subtract))
                    then(ts(lb1[:, :, l, :], lb[:, :, l, :], -1.0, 1.0, ALU.mult, ALU.add))

            def ada():
                per = L * ADA_CHUNKS // ADA_SLOTS
                flat = mod[:, :, :, :].rearrange("p l c s -> p (l c) s")
                with dve.Fori(0, per) as i:
                    for s in range(ADA_SLOTS):
                        n = use["ada", s % 2][1]
                        dve.wait_ge(ps_full[s % 2], i * 3 + (n + s // 2))
                        nc.vector.tensor_copy(flat[:, bass.ds(i * 24 + 4 * s, 4), :],
                                              ps[s % 2][:, 0:8].rearrange("p (j s) -> p j s", s=2))\
                            .then_inc(ps_free[s % 2], 1)
                for b in range(2):
                    dve.wait_ge(ps_free[b], use["ada", b][1] - 1 + 3 * per)
                for l in range(L):
                    bias = sm(l, "ada_b", 0, 72).unsqueeze(2).broadcast_to([P, 72, 2])
                    then(tt(mod[:, l, :, :], mod[:, l, :, :], bias, ALU.add))
                for l in range(L):
                    for w, name in enumerate(("ffn1_norm", "mix_norm", "ffn2_norm")):
                        at = 3 * w * DT
                        gain = sm(l, name, 0, DT).unsqueeze(2).broadcast_to([P, DT, 2])
                        then(stt(gain_s[:, l, w, :, :], mod[:, l, at + DT:at + 2 * DT, :], 1.0, gain, ALU.add, ALU.mult))
                        do(ts(gate_s[:, l, w, :, :], mod[:, l, at + 2 * DT:at + 3 * DT, :], 1.0 if w == 1 else 0.5,
                              None, ALU.mult), coef.of(0) if (l, w) == (L - 1, 2) else None)

            def norm(l, w):
                W = widths[l, w]
                dve.wait_ge(*freed(("stat", l, w)))
                then(nc.vector.reciprocal(root[:, 0:W], root[:, 0:W]))
                if (l, w) == (0, 0):
                    dve.wait_ge(x_in, 32)
                for d in range(DT):
                    do(tt(hT[:, d, 0:W], xT[:, d, 0:W], root[:, 0:W], ALU.mult), scaled.of((l, w, d)))

            def add_to_x(l, w, key, d, W):
                src = full(dve, key)
                for st in range(W // S):
                    cols = slice(st * S, (st + 1) * S)
                    do(stt(xT[:, d, cols], src[:, cols], gate_s[:, l, w, d, st:st + 1], xT[:, d, cols], ALU.mult, ALU.add),
                       freed(key) if st == W // S - 1 else None)

            def ffn(l, f):
                W = widths[l, 2 * f]
                with dve.Fori(0, FT // 2) as i:
                    for s in range(2):
                        na, nb = use["up", l, f, 2 * s][1], use["up", l, f, 2 * s + 1][1]
                        dve.wait_ge(ps_free[2 * s], i + na)
                        dve.wait_ge(ps_full[2 * s + 1], i + nb)
                        tt(g_ff[:, bass.ds(i * 2 + s, 1), 0:W].rearrange("p o t -> p (o t)"), silu_ff[:, s, 0:W],
                           ps[2 * s + 1][:, 0:W], ALU.mult).then_inc(ps_free[2 * s + 1], 1)
                for d in range(DT):
                    add_to_x(l, 2 * f, ("down", l, f, d), d, W)

            def level_views(a, m):
                v = a.rearrange("p h (n two m) -> p h n two m", two=2, m=m)
                return v[:, :, :, 0, :], v[:, :, :, 1, :]

            def level_diff(l, n):
                W, m, hs = out_w[l], LEVELS[n % len(LEVELS)], slice(2 * (n // len(LEVELS)), 2 * (n // len(LEVELS)) + 2)
                buf = lev[n % 3]
                if m == 0:
                    do(tt(buf[:, 1, :, 0:W], kd[0][:, hs, 0:W], kd[1][:, hs, 0:W], ALU.add), diffs.of((l, n)))
                    return
                f0, f1 = level_views(bd[0][:, hs, 0:W], m)
                g0, g1 = level_views(bd[1][:, hs, 0:W], m)
                q0, q1 = level_views(buf[:, 0, :, 0:W], m)
                k0, k1 = level_views(buf[:, 1, :, 0:W], m)
                rf = f0[:, :, :, m - 1:m].broadcast_to(list(f0.shape))
                rg = g1[:, :, :, 0:1].broadcast_to(list(g1.shape))
                do(tt(q1, f1, rf, ALU.subtract))
                do(tt(k0, rf, f0, ALU.subtract))
                do(tt(q0, g0, rg, ALU.subtract))
                do(tt(k1, rg, g1, ALU.subtract), diffs.of((l, n)))

            def level_weigh(l, n):
                W, m, hs = out_w[l], LEVELS[n % len(LEVELS)], slice(2 * (n // len(LEVELS)), 2 * (n // len(LEVELS)) + 2)
                buf = lev[n % 3]
                if m == 0:
                    return
                decays.wait(dve, (l, n))
                k0, k1 = level_views(buf[:, 1, :, 0:W], m)
                f0, _ = level_views(kd[0][:, hs, 0:W], m)
                _, g1 = level_views(kd[1][:, hs, 0:W], m)
                do(tt(k0, k0, f0, ALU.mult))
                do(tt(k1, k1, g1, ALU.mult))
                do(tt(buf[:, 0, :, 0:W], buf[:, 0, :, 0:W], q[:, hs, 0:W], ALU.mult), weighted.of((l, n)))

            def level_take(l, n):
                nc_, li = out_w[l] // P, n % len(LEVELS)
                do.settle()
                for hh in range(2):
                    h = 2 * (n // len(LEVELS)) + hh
                    key = ("lev", l, n, hh)
                    src = full(dve, key)[:, 0:nc_ * P].rearrange("p (c t) -> p c t", t=P)
                    if li == 0:
                        do(nc.vector.tensor_copy(attn[:, h, 0:nc_, :], src), freed(key))
                    else:
                        mask = masks[:, li:li + 1, :].broadcast_to([P, nc_, P])
                        do(nc.vector.copy_predicated(attn[:, h, 0:nc_, :], mask, src), freed(key))

            def mixer_in(l):
                W = out_w[l]
                for n in range(8):
                    dr, j = n // 4, n % 4
                    dve.wait_ge(*freed((("zf", "zb")[dr], l, j)))
                    k, b = kd[dr][:, j, :], bd[dr][:, j, :]
                    then(ts(k, k, lb1[:, dr, l, j:j + 1], lb[:, dr, l, j:j + 1], ALU.mult, ALU.add))
                    do(ts(b, k, TINY, None, ALU.max))
                    then(ts(split[:, dr, j, :], k, 1.0 / TINY, 1.0, ALU.mult, ALU.min), f_split.of((l, n)))
                    do(ts(k, k, -1.0, 1.0, ALU.mult, ALU.add))
                for j in range(4):
                    dve.wait_ge(*freed(("q", l, j)))
                    do(ts(q[:, j, 0:W], q[:, j, 0:W], DK ** -0.5, None, ALU.mult))
                for n in range(8):
                    dr, j = n // 4, n % 4
                    logged.wait(dve, (l, n))
                    b = bd[dr][:, j, :]
                    then(tt(b, b, split[:, dr, j, :], ALU.add))
                    for c in range(CH):
                        v = b[:, c * P:(c + 1) * P]
                        if dr:
                            v = v[:, ::-1]
                        do(nc.vector.tensor_tensor_scan(v, ones[1][:, :], v, 0.0, ALU.mult, ALU.add))
                do.settle()
                level_diff(l, 0)
                for n in range(NLEV):
                    if n:
                        level_take(l, n - 1)
                    if n + 1 < NLEV:
                        level_diff(l, n + 1)
                    level_weigh(l, n)
                    if n < 12:
                        dve.wait_ge(*freed(("hy", l, n)))
                        for tap, lo in ((0, 0), (2, 2)):
                            do.settle()
                            for st in range(W // S):
                                cols = slice(st * S, (st + 1) * S)
                                do(stt(uc[:, n, cols], upad[:, n % 2, st, lo:lo + S], sm(l, "conv_w", 12 * tap + n),
                                       uc[:, n, cols], ALU.mult, ALU.add),
                                   conv_done.of((l, n)) if tap and st == W // S - 1 else None)
                level_take(l, NLEV - 1)

            def hgrn_out(l):
                W = out_w[l]
                seq = ((2, 3, 0), (3, 2, 1))
                for dr in range(2):
                    at = P - 1 if dr == 0 else 0
                    v = bd[dr].rearrange("p h (c t) -> p (h c) t", t=P)
                    tv = tail[dr].rearrange("p h (c t) -> p (h c) t", t=P)
                    do(tt(tv, v[:, :, at:at + 1].broadcast_to([P, 16, P]), v, ALU.subtract), tail_diff.of((l, dr)))
                for dr in range(2):
                    at = P - 1 if dr == 0 else 0
                    tail_exp.wait(dve, (l, dr))
                    do(tt(kd[dr], kd[dr], tail[dr], ALU.mult), k_decayed.of((l, dr)))
                    v = bd[dr].rearrange("p h (c t) -> p (h c) t", t=P)
                    then(nc.vector.tensor_copy(elast[:, dr, :].unsqueeze(2), v[:, :, at:at + 1]))
                    do(tt(bd[dr][:, :, 0:W], bd[dr][:, :, 0:W], q[:, :, 0:W], ALU.mult), q_decayed.of((l, dr)))
                for j in range(3):
                    for dr in range(2):
                        src = full(dve, ("st", l, j, dr))
                        do.settle()
                        if j == 0:
                            do(nc.vector.tensor_copy(state[dr][:, 0, :], src[:, :]), freed(("st", l, j, dr)))
                        else:
                            for h in range(H):
                                col = h * CH + seq[dr][j]
                                hc = slice(h * P, (h + 1) * P)
                                do(stt(state[dr][:, j, hc], state[dr][:, j - 1, hc], elast[:, dr, col:col + 1], src[:, hc],
                                       ALU.mult, ALU.add), freed(("st", l, j, dr)) if h == H - 1 else None)
                for h in range(H):
                    dve.wait_ge(*freed(("ostat", l, h)))
                    then(nc.vector.reciprocal(o_root[:, h, 0:W], o_root[:, h, 0:W]))
                    then(tt(o_raw[:, h, 0:W], o_raw[:, h, 0:W], o_root[:, h, 0:W], ALU.mult))
                    do(stt(ya[:, h, 0:W], o_raw[:, h, 0:W], sm(l, "hg_out_norm"), ya[:, h, 0:W], ALU.mult, ALU.mult),
                       ya_done.of((l, h)))

            def hyena(l):
                W = out_w[l]
                for i, name in enumerate(("b1", "b2", "b3")):
                    src = full(dve, ("mlp", l, i))
                    then(ts(arg, src[0:FH, 0:S], sm(l, name, p=FH), sm(l, "freq", p=FH), ALU.add, ALU.mult),
                         freed(("mlp", l, i)))
                    then(ts(turns, arg, 1.0 / TWO_PI, ROUND, ALU.mult, ALU.add))
                    then(ts(turns, turns, ROUND, None, ALU.subtract))
                    for part in (PI_A, PI_B, PI_C):
                        then(stt(arg, turns, -part, arg, ALU.mult, ALU.add))
                    do(ts(arg, arg, 3.1415925, -3.1415925, ALU.min, ALU.max), phase.of((l, i)))
                dve.wait_ge(hy_in, 32 * (l + 1))
                for t in range(2):
                    for cc in range(4):
                        src = full(dve, ("tap", l, t, cc))
                        do(tt(taps[:, t, cc, :], src[:, :], window[:, cc // 2, t, :], ALU.mult), freed(("tap", l, t, cc)))
                do.settle()
                for t in range(2):
                    do(tt(even_odd[:, 0, t, :, :], taps[:, t, 0:2, :], taps[:, t, 2:4, :], ALU.add))
                    do(tt(even_odd[:, 1, t, :, :], taps[:, t, 0:2, :], taps[:, t, 2:4, :], ALU.subtract),
                       taps_ready.of(l) if t else None)
                src = full(dve, ("l1", l))
                then(nc.vector.reciprocal(rnorm[:, :], src[:, 0:8]), freed(("l1", l)))
                then(ts(rnorm[:, :], rnorm[:, :], 2.0 / 512, None, ALU.mult))
                for o in range(2):
                    for st in range(W // S):
                        for f in range(2):
                            if f == 0 and st == 0:
                                dve.wait_ge(*freed(("kf", l, 1, 1, 1)))
                            kp, kq = spectrum[:, o, f, 0, :], spectrum[:, o, f, 1, :]
                            a = full(dve, ("fw", l, o, st, f, 0))
                            do.settle()
                            do(tt(prod[:, 0, :], a[:, :], kp, ALU.mult))
                            do(tt(prod[:, 1, :], a[:, :], kq, ALU.mult), freed(("fw", l, o, st, f, 0)))
                            b = full(dve, ("fw", l, o, st, f, 1))
                            do(tt(prod[:, 2, :], b[:, :], kq, ALU.mult))
                            then(tt(prod[:, 3, :], b[:, :], kp, ALU.mult), freed(("fw", l, o, st, f, 1)))
                            do(tt(spec_y[st][:, f, 0, :], prod[:, 0, :], prod[:, 2, :], ALU.subtract))
                            do(tt(spec_y[st][:, f, 1, :], prod[:, 1, :], prod[:, 3, :], ALU.add), spect.of((l, o, st, f)))
                    do.settle()
                    for ct in range(CT):
                        z, t = yb[:, ct, 0:W], prod[:, ct, 0:W]
                        src = full(dve, ("inv", l, o, ct))
                        then(ts(t, z, sm(l, "skip", o * CT + ct), None, ALU.mult))
                        then(stt(t, src[:, 0:W], rnorm[:, o * CT + ct:o * CT + ct + 1], t, ALU.mult, ALU.add),
                             freed(("inv", l, o, ct)))
                        do(tt(z, t, uc[:, o * CT + ct, 0:W], ALU.mult), z_done.of((l, o, ct)))

            def mla(l):
                W = out_w[l]
                for j, (n, width, p, name) in enumerate(((2, W, P, "q_a_norm"), (1, T, P, "kv_a_norm"), (1, T, ROPE, "k_rope_norm"))):
                    dve.wait_ge(*freed(("ms", l, 0, j)))
                    r = m_root[0:p, j, 0:width]
                    then(nc.vector.reciprocal(r, r))
                    for i in range(n):
                        dst = kr if j == 2 else lora[:, 2 * j + i, 0:width]
                        do(stt(dst, raw[0:p, (0, 2, 3)[j] + i, 0:width], sm(l, name, i, 1, p), r, ALU.mult, ALU.mult),
                           m_normed.of((l, 0, j)) if i == n - 1 else None)
                for bt, (name, dst) in enumerate((("q_nope_norm", qn), ("q_rope_norm", qr), ("k_nope_norm", kn)), 1):
                    p = ROPE if bt == 2 else P
                    width = T if bt == 3 else W
                    for h in range(H):
                        dve.wait_ge(*freed(("ms", l, bt, h)))
                        r = m_root[0:p, h, 0:width]
                        then(nc.vector.reciprocal(r, r))
                        do(stt(dst[:, h, 0:width], m_raw[0:p, h, 0:width], sm(l, name, 0, 1, p), r, ALU.mult, ALU.mult),
                           m_normed.of((l, bt, h)))
                for i in range(5):
                    x = qr[:, i, 0:S] if i < 4 else kr[:, 0:S]
                    src = full(dve, ("rope", l, i))
                    do.settle()
                    do(tt(rope_t, src[0:ROPE, 0:S], sinT, ALU.mult), freed(("rope", l, i)))
                    then(tt(x, x, cosT, ALU.mult))
                    do(tt(x, x, rope_t, ALU.add), roped.of((l, i)))
                n = len(tiles[l])
                for i in range(n + 1):
                    if i < n:
                        nk = T if tiles[l][i][0] < 2 else S
                        src = full(dve, ("sc", l, i))
                        do.settle()
                        then(nc.vector.reduce_max(mxt[:, i % 4, 0:1], src[:, 0:nk], AX.X))
                        do(ts(mxt[:, i % 4, 1:2], mxt[:, i % 4, 0:1], -SCALE, None, ALU.mult), row_max.of((l, i)))
                    if i:
                        nk = T if tiles[l][i - 1][0] < 2 else S
                        s = (i - 1) % 4
                        exped.wait(dve, (l, i - 1))
                        then(nc.vector.reciprocal(mxt[:, s, 3:4], mxt[:, s, 2:3]), freed(("sc", l, i - 1)))
                        do(ts(prob[:, s, 0:nk], prob[:, s, 0:nk], mxt[:, s, 3:4], None, ALU.mult), prob_ready.of((l, i - 1)))

            def merge(l):
                W = out_w[l]
                for br in range(3):
                    for d in range(DT):
                        dve.wait_ge(*freed(("gate", l, br, d)))
                        src = full(dve, ("br", l, br, d))
                        g = gate_t[:, (br * DT + d) % 2, 0:W]
                        if br == 0:
                            do(tt(mix[:, d, 0:W], src[:, 0:W], g, ALU.mult), freed(("br", l, br, d)))
                        else:
                            t = part_t[:, d % 2, 0:W]
                            then(tt(t, src[:, 0:W], g, ALU.mult), freed(("br", l, br, d)))
                            do(tt(mix[:, d, 0:W], mix[:, d, 0:W], t, ALU.add), mixed.of((l, d)) if br == 2 else None)
                for d in range(DT):
                    add_to_x(l, 1, ("out", l, d), d, W)

            setup()
            ada()
            for l in range(L):
                norm(l, 0)
                ffn(l, 0)
                norm(l, 1)
                mixer_in(l)
                hgrn_out(l)
                hyena(l)
                mla(l)
                merge(l)
                norm(l, 2)
                ffn(l, 1)


def shape_tables():
    f32 = np.float32
    fixed = np.zeros((P, NFIXED), f32)
    fixed[:, 0:128] = np.eye(P)
    inv = (f32(10000.0) ** (-np.arange(0, 32, 2, dtype=f32) / f32(32))).astype(f32)
    row = np.repeat(np.arange(S // 64, dtype=f32), 64)
    col = np.tile(np.arange(64, dtype=f32), S // 64)
    ang = [(v[:, None] * inv).astype(f32).T for v in (row, col)]
    ang = np.concatenate([ang[0], ang[0], ang[1], ang[1]]).astype(np.float64)
    fixed[0:ROPE, 128:384], fixed[0:ROPE, 384:640] = np.cos(ang), np.sin(ang)
    for base in (0, 32):
        for j in range(16):
            fixed[base + 16 + j, 640 + base + j] = -1.0
            fixed[base + j, 640 + base + 16 + j] = 1.0
    t = np.linspace(0.0, 1.0, S, dtype=f32)[:, None]
    w = (f32(2.0 * math.pi / S) * np.arange(S, dtype=f32))[:, None]
    bands = np.linspace(1e-4, 15, 16, dtype=f32)[None, :]
    arg = (bands * w).astype(np.float64)
    fixed[0:EMB, 704:960] = np.concatenate([t, np.cos(arg), -np.sin(arg)], axis=-1).T
    om = 2 * np.pi * (np.arange(S) + 0.5) / 512
    ph = np.arange(S)[:, None] * om[None, :]
    mats = [np.cos(ph), np.sin(ph), np.cos(ph).T, np.sin(ph).T]
    deltas = np.abs(np.linspace(math.log(1e-2) / 1.5, math.log(1e-2) / 0.3, HYW, dtype=f32))
    win = np.exp(-t.astype(np.float64) * deltas) + 0.05
    win_b = win.copy()
    win_b[0] = 0.0
    tab = np.concatenate([m.reshape(2, P, -1).transpose(1, 0, 2).reshape(P, -1) for m in mats + [win, win_b]], 1)
    s, tq = np.arange(P)[:, None], np.arange(P)[None, :]
    masks = np.stack([s == tq] + [(s // (2 * m) == tq // (2 * m)) & (s // m != tq // m) for m in LEVELS[1:]])
    return fixed, tab.astype(f32), np.ascontiguousarray(masks.transpose(1, 0, 2).astype(np.int32))


def lay_out(v):
    def cols(a):
        a = a.reshape(a.shape[:-1] + (-1, P))
        return np.swapaxes(a, -1, -2)

    def chunks(w, width):
        n_l, rows, n = w.shape
        return w.reshape(n_l, rows // P, P, n // width, width).transpose(0, 3, 2, 1, 4)

    out = {}
    out["cT"] = np.stack([cols(v["c"][0]), cols(v["c_ctx"])], -1)
    x = np.concatenate([v["x"][0], v["ctx"][0]], 0)
    out["xT"] = x.T.reshape(DT, P, T).transpose(1, 0, 2)
    out["ada"] = chunks(v["ada_w"], 512).reshape(L * ADA_CHUNKS, P, 8, 512)
    for f, (a, b) in enumerate((("ffn1_w13", "ffn1_w2"), ("ffn2_w13", "ffn2_w2"))):
        w = v[a].reshape(L, DT, P, 2, FT, P).transpose(0, 4, 2, 3, 1, 5)
        out[f"up{f}"] = w.reshape(L, FT, P, UP_CHUNK)
        out[f"down{f}"] = chunks(v[b], P).reshape(L, DT, P, DOWN_CHUNK)
    w = v["w_in"]
    parts = [w[:, :, 512:1024], w[:, :, 1024:1536], w[:, :, 0:512], w[:, :, 1536:4352]]
    out["proj"] = np.concatenate([chunks(p, 256) for p in parts], 1).reshape(L, 17, P, PROJ_CHUNK)
    out["kvkr"] = chunks(w[:, :, 4352:4544], 192).reshape(L, 1, P, KVKR_CHUNK)
    uq = v["w_uq"].reshape(L, 2, P, 768).transpose(0, 2, 1, 3).reshape(L, P, 1536)
    out["mla"] = np.concatenate([uq, v["w_ukv"]], -1)[:, None]
    merge = []
    for i, name in enumerate(("w_br_a", "w_br_b", "w_br_c")):
        gate = chunks(w[:, :, 4544 + i * D:4544 + (i + 1) * D], 256).reshape(L, 4, P, 2048)
        merge.append(np.concatenate([gate, chunks(v[name], 256).reshape(L, 4, P, 1024)], -1))
    out["merge"] = np.concatenate(merge, 1)
    out["wout"] = chunks(v["w_out"], 256).reshape(L, 4, P, PROJ_CHUNK)
    out["w4"] = v["hy_w4"]
    out["logits"] = v["hg_lb_logits"].reshape(2, L, H, P).transpose(3, 0, 1, 2)
    small = np.zeros((P, L, NSMALL), np.float32)

    def put(name, a):
        at, n = SMALL[name]
        small[0:a.shape[1], :, at:at + n] = np.swapaxes(a, 0, 1)
    for name in ("ffn1_norm", "mix_norm", "ffn2_norm", "ada_b", "hg_out_norm", "q_a_norm", "kv_a_norm",
                 "q_nope_norm", "k_nope_norm"):
        put(name, cols(v[name]))
    put("conv_w", cols(v["hy_conv_w"].reshape(L, -1)))
    put("conv_b", cols(v["hy_conv_b"]))
    put("skip", cols(v["hy_skip"].reshape(L, -1)))
    for name, src in (("b1", "hy_b1"), ("b2", "hy_b2"), ("b3", "hy_b3"), ("freq", "hy_freq"),
                      ("q_rope_norm", "q_rope_norm"), ("k_rope_norm", "k_rope_norm")):
        put(name, v[src][:, :, None])
    for name in ("w1", "w2", "w3"):
        put(name, v["hy_" + name])
    out["small"] = small
    out["fixed"], out["hy_tab"], out["masks"] = shape_tables()
    return {k: np.ascontiguousarray(a) for k, a in out.items()}


def kernel(**inputs):
    import concourse.bacc as bacc
    from concourse.bass_utils import run_bass_kernel_spmd as run

    arrays = lay_out({k: np.asarray(a) for k, a in inputs.items()})
    nc = bacc.Bacc("TRN2", target_bir_lowering=False, num_devices=1)
    dram = {k: nc.dram_tensor(f"in_{k}", a.shape, mybir.dt.from_np(a.dtype), kind="ExternalInput").ap()
            for k, a in arrays.items()}
    out = nc.dram_tensor("out_0", (P, DT, S), mybir.dt.float32, kind="ExternalOutput").ap()
    build(nc, dram, out)
    r = run(nc, [{f"in_{k}": a for k, a in arrays.items()}], core_ids=[0])
    got = r.results[0]["out_0"]
    return np.ascontiguousarray(got.transpose(1, 0, 2).reshape(D, S).T)[None]
```

```python
import math
from contextlib import ExitStack

import concourse.bass as bass
import numpy as np
from concourse import mybir

P = 128
D, T, S, L = 1024, 512, 256, 2
DT = D // P
FF = 2816
FT = FF // P
NMOD = 9
H = 4
DK = 128
CH = T // P
QK = 192
ROPE = 64
EPS = 1e-6
HYW, FH, EMB = 512, 64, 33
CT = HYW // P
MLP_AT = (9, 11, 13)
LEVELS = [0, 64, 32, 16, 8, 4, 2, 1]
SCALE = QK ** -0.5
TINY = 2.0 ** -62
TWO_PI = 2.0 * math.pi
PI_A, PI_B = 6.28125, 0.00193500518798828125
PI_C = TWO_PI - PI_A - PI_B
ROUND = 1.5 * 2.0 ** 23
UP_CHUNK, DOWN_CHUNK, PROJ_CHUNK = 8 * 256, FT * P, 8 * 256
KVKR_CHUNK, MLA_CHUNK, MERGE_CHUNK = 8 * 192, 2 * 768 + 1024, 8 * 256 + 4 * 256
SLOT = max(UP_CHUNK, DOWN_CHUNK, MERGE_CHUNK, MLA_CHUNK)
MOD_TILES = NMOD * D // P
FIRST = 2 * DT
ADA_PLAN = {(0, 0): (0, FIRST, (3, 2)), (0, 1): (1, 0, (3, 3))}
ADA_REST = {k: MOD_TILES - first - FT // 2 * sum(g) for k, (_, first, g) in ADA_PLAN.items()}

SMALL = {}
_at = 0
for _name, _n in (("ffn1_norm", 8), ("mix_norm", 8), ("ffn2_norm", 8), ("ada_b", 72), ("hg_out_norm", 1),
                  ("conv_w", 36), ("conv_b", 12), ("b1", 1), ("b2", 1), ("b3", 1), ("freq", 1), ("skip", 8),
                  ("q_a_norm", 2), ("kv_a_norm", 1), ("q_nope_norm", 1), ("q_rope_norm", 1),
                  ("k_nope_norm", 1), ("k_rope_norm", 1), ("w1", FH), ("w2", FH), ("w3", FH)):
    SMALL[_name] = (_at, _n)
    _at += _n
NSMALL = _at
FIXED = {"ident": (0, 128), "cos": (128, 256), "sin": (384, 256), "perm": (640, 64), "emb": (704, 256)}
NFIXED = 960


class Signal:

    def __init__(self, sem, keys):
        self.sem, self.value, self.made = sem, {k: i + 1 for i, k in enumerate(keys)}, 0

    def wait(self, eng, key):
        eng.wait_ge(self.sem, self.value[key])

    def of(self, key):
        self.made += 1
        assert self.value[key] == self.made, (key, self.made)
        return self.sem, self.made


class Steps:

    def __init__(self, eng, sem):
        self.eng, self.sem, self.n, self.last = eng, sem, 0, None

    def __call__(self, ins, event=None):
        if event is None:
            self.n += 1
            event = (self.sem, self.n)
        ins.then_inc(event[0], 1)
        self.last = event

    def settle(self):
        if self.last:
            self.eng.wait_ge(*self.last)


def build(nc, dram, out):
    F32 = mybir.dt.float32
    ACT, ALU, AX = mybir.ActivationFunctionType, mybir.AluOpType, mybir.AxisListType
    with ExitStack() as ctx:
        def sb(name, shape, dt=F32):
            return ctx.enter_context(nc.sbuf_tensor(name, shape, dt))

        def sem(name):
            return ctx.enter_context(nc.semaphore(name))

        xT = sb("xT", [P, DT, T])
        hT = sb("hT", [P, DT, T])
        ring = sb("ring", [P, 2, SLOT])
        fixed = sb("fixed", [P, NFIXED])
        masks = sb("masks", [P, len(LEVELS), P], mybir.dt.int32)
        small = sb("small", [P, L, NSMALL])
        mod = sb("mod", [P, L, 72, 2])
        gain_s = sb("gain_s", [P, L, 3, DT, 2])
        gate_s = sb("gate_s", [P, L, 3, DT, 2])
        logits = sb("logits", [P, 2, L, H])
        lb_e = sb("lb_e", [P, 2, L, H])
        lb_t = sb("lb_t", [P, 2, 2, H])
        lb = sb("lb", [P, 2, L, H])
        lb1 = sb("lb1", [P, 2, L, H])
        ones = {n: sb(f"ones{n}", [P, P]) for n in (1, 1024, 256, 128, 64)}
        eps_t = sb("eps_t", [P, 1])
        ada_acc = sb("ada_acc", [P, 2, 3, 2])
        root = sb("root", [P, T])
        rnorm = sb("rnorm", [P, 8])
        elast = sb("elast", [P, 2, 16])
        mxt = sb("mxt", [P, 4, 4])
        R = sb("R", [P, 16 * 2048 + 1040])

        def unit(u, shape, off=0, p=P):
            n = int(np.prod(shape))
            a = R[0:p, u * 2048 + off:u * 2048 + off + n]
            if len(shape) == 2:
                return a.rearrange("p (a b) -> p a b", b=shape[1])
            if len(shape) == 3:
                return a.rearrange("p (a b c) -> p a b c", b=shape[1], c=shape[2])
            if len(shape) == 4:
                return a.rearrange("p (a b c d) -> p a b c d", b=shape[1], c=shape[2], d=shape[3])
            return a

        ada_first = unit(0, (FIRST, D))
        ada_buf = [R[:, 8 * 2048 + g * 3072:8 * 2048 + (g + 1) * 3072].rearrange("p (n d) -> p n d", d=D) for g in range(2)]
        c_row = unit(13, (2, D))
        ada_prod = unit(14, (4, D))
        g_ff = unit(0, (FT, T))
        silu_ff = unit(6, (2, T))
        q = unit(0, (H, T))
        kd = [unit(1, (H, T)), unit(2, (H, T))]
        bd = [unit(3, (H, T)), unit(4, (H, T))]
        attn = unit(5, (H, CH, P))
        split = unit(6, (2, H, T))
        lev = [unit(6 + i, (2, 2, T)) for i in range(3)]
        val = unit(9, (CH, HYW))
        ya = unit(10, (H, T))
        tail = [unit(6, (H, T)), unit(7, (H, T))]
        kdT = [unit(6, (3, 512)), unit(7, (3, 512))]
        state = [unit(8, (3, 512)), unit(15, (3, 512))]
        o_raw, o_sq, o_root = unit(1, (H, T)), unit(2, (H, T)), unit(0, (H, T))
        uc = unit(11, (3 * CT, T))
        upad = unit(16, (2, 2, S + 2))
        spectrum = unit(0, (2, 2, 2, HYW))
        hy_tab = unit(3, (4096,))
        dft = hy_tab[:, 0:2048].rearrange("p (m t f) -> p m t f", m=4, t=2)
        window = hy_tab[:, 2048:4096].rearrange("p (w t c) -> p w t c", w=2, t=2)
        w4 = unit(5, (4 * HYW,), p=FH)
        taps = unit(6, (2, 4, HYW))
        even_odd = unit(8, (2, 2, 2, HYW))
        zt = unit(2, (CH, HYW))
        arg, turns = root[0:FH, 0:S], root[0:FH, S:2 * S]
        hid = unit(15, (S,), 1536, FH)
        prod = unit(15, (4, HYW))
        spec_y = [unit(5, (2, 2, HYW)), unit(6, (2, 2, HYW))]
        yb = unit(13, (CT, T))
        raw = unit(14, (4, T))
        qn, qr, kn = unit(0, (H, T)), unit(1, (H, T), 0, ROPE), unit(2, (H, T))
        kr = unit(3, (T,), 0, ROPE)
        rope_t = unit(3, (S,), 512, ROPE)
        vv = unit(4, (CH, 512))
        lora = unit(5, (3, T))
        m_sq, m_root, m_raw = unit(6, (4, T)), unit(7, (4, T)), unit(9, (4, T))
        prob = unit(12, (4, T))
        probT = unit(8, (2, CH, P))
        yc = unit(11, (H, T))
        mix = unit(0, (DT, T))
        gate_t = unit(2, (2, T))
        part_t = unit(3, (2, T))

        ps = [ctx.enter_context(nc.psum_tensor(f"ps{i}", [P, 512], F32)) for i in range(8)]

        ident = fixed[:, 0:128]
        cosT, sinT = fixed[0:ROPE, 128:384], fixed[0:ROPE, 384:640]
        perm, emb = fixed[0:ROPE, 640:704], fixed[0:EMB, 704:960]

        def sm(l, name, j=0, n=1, p=P):
            at = SMALL[name][0] + j
            return small[0:p, l, at:at + n]

        ps_full = [sem(f"ps_full{i}") for i in range(8)]
        ps_free = [sem(f"ps_free{i}") for i in range(8)]
        landed = [sem("weights0"), sem("weights1")]
        ada_landed, ada_used = [sem("ada_landed0"), sem("ada_landed1")], [sem("ada_used0"), sem("ada_used1")]
        ada_first_in, c_in = [sem(f"ada_first_in{i}") for i in range(4)], sem("c_in")
        tables_in = sem("tables_in")
        mod_written = sem("mod_written")
        params_in, x_in, hy_in, y_out = sem("params_in"), sem("x_in"), sem("hy_in"), sem("y_out")
        LW = [(l, w) for l in range(L) for w in range(3)]
        widths = {(l, w): (T if l < L - 1 or w < 2 else S) for l, w in LW}
        out_w = [T if l < L - 1 else S for l in range(L)]

        def signal(name, keys):
            return Signal(sem(name), list(keys))
        c_silu = signal("c_silu", [0, 1])
        consts = signal("consts", [0])
        lb_max = signal("lb_max", [0])
        lb_exp = signal("lb_exp", [0])
        squared = signal("squared", [(l, w, d) for l, w in LW for d in range(DT)])
        scaled = signal("scaled", [(l, w, d) for l, w in LW for d in range(DT)])
        h_ready = signal("h_ready", [(l, w, d) for l, w in LW for d in range(DT)])
        h_ctx_ready = signal("h_ctx_ready", [(l, w, d) for l, w in LW for d in range(DT) if widths[l, w] == T])
        f_split = signal("f_split", [(l, n) for l in range(L) for n in range(8)])
        logged = signal("logged", [(l, n) for l in range(L) for n in range(8)])
        conv_done = signal("conv_done", [(l, j) for l in range(L) for j in range(12)])
        NLEV = 2 * len(LEVELS)
        LN = [(l, n) for l in range(L) for n in range(NLEV)]
        diffs = signal("diffs", LN)
        decays = signal("decays", [(l, n) for l, n in LN if n % len(LEVELS)])
        weighted = signal("weighted", [(l, n) for l, n in LN if n % len(LEVELS)])
        LDIR = [(l, d) for l in range(L) for d in range(2)]
        tail_diff = signal("tail_diff", LDIR)
        tail_exp = signal("tail_exp", LDIR)
        k_decayed = signal("k_decayed", LDIR)
        q_decayed = signal("q_decayed", LDIR)
        ya_done = signal("ya_done", [(l, h) for l in range(L) for h in range(H)])
        phase = signal("phase", [(l, i) for l in range(L) for i in range(3)])
        hidden = signal("hidden", [(l, i) for l in range(L) for i in range(3)])
        taps_ready = signal("taps_ready", range(L))
        taps_abs = signal("taps_abs", range(L))
        LO = [(l, o) for l in range(L) for o in range(2)]
        spect = signal("spect", [(l, o, st, f) for l, o in LO for st in range(out_w[l] // S) for f in range(2)])
        z_done = signal("z_done", [(l, o, st, c) for l, o in LO for st in range(out_w[l] // S) for c in range(CT // 2)])
        BATCH = [(l, b, j) for l in range(L) for b in range(4) for j in range(3 if b == 0 else 4)]
        m_squared = signal("m_squared", BATCH)
        m_normed = signal("m_normed", BATCH)
        roped = signal("roped", [(l, i) for l in range(L) for i in range(5)])
        tiles = {l: [(qt, h) for qt in range(out_w[l] // P) for h in range(H)] for l in range(L)}
        SC = [(l, i) for l in range(L) for i in range(len(tiles[l]))]
        row_max = signal("row_max", SC)
        exped = signal("exped", SC)
        prob_ready = signal("prob_ready", SC)
        mixed = signal("mixed", [(l, d) for l in range(L) for d in range(DT)])
        vector_steps, scalar_steps = sem("vector_steps"), sem("scalar_steps")

        chunk_at, order = {}, []
        for l in range(L):
            for key, n in (("up0", 22), ("down0", 8), ("proj", 17), ("kvkr", 1), ("mla", 1), ("merge", 12),
                           ("out", 4), ("up1", 22), ("down1", 8)):
                chunk_at[l, key] = len(order)
                order += [(l, key, j) for j in range(n)]
        released = {}
        use = {}
        bank_uses = [0] * 8
        rr = [0]

        block = ctx.enter_context(nc.Block())

        @block.tensor
        def _(pe):
            mm = nc.tensor.matmul

            def bank(key, b=None):
                if b is None:
                    b = rr[0] % 8
                    rr[0] += 1
                if bank_uses[b]:
                    pe.wait_ge(ps_free[b], bank_uses[b])
                bank_uses[b] += 1
                use[key] = (b, bank_uses[b])
                return b

            def taken(key):
                b, n = use[key]
                pe.wait_ge(ps_free[b], n)

            def weights(c):
                pe.wait_ge(landed[c % 2], 16 * (c // 2 + 1))
                return ring[:, c % 2, :]

            def used(c, key):
                released[c] = use[key]

            def warm():
                consts.wait(pe, 0)
                for b in range(8):
                    mm(ps[b][:, 0:P], ones[1][:, :], ones[1][:, :], start=True, stop=True).then_inc(ps_full[b], 1)
                    bank_uses[b] += 1

            def norm(l, w):
                W = widths[l, w]
                b = bank(("stat", l, w))
                for d in range(DT):
                    squared.wait(pe, (l, w, d))
                    last = mm(ps[b][:, 0:W], ones[1024][:, :], hT[:, d, 0:W], start=d == 0, stop=d == DT - 1)
                last.then_inc(ps_full[b], 1)

            def ffn(l, f):
                w = 2 * f
                W = widths[l, w]
                c0 = chunk_at[l, f"up{f}"]
                h_ready.wait(pe, (l, w, DT - 1))
                if W == T:
                    h_ctx_ready.wait(pe, (l, w, DT - 1))
                base = list(bank_uses)
                with pe.Fori(0, FT // 2) as i:
                    for s in range(2):
                        c = c0 + s
                        pe.wait_ge(landed[c % 2], i * 16 + 16 * (c // 2 + 1))
                        wt = ring[:, c % 2, 0:UP_CHUNK].rearrange("p (ab k n) -> p ab k n", ab=2, k=DT)
                        for ab in range(2):
                            b = 2 * s + ab
                            pe.wait_ge(ps_free[b], i + base[b])
                            for k in range(DT):
                                last = mm(ps[b][:, 0:W], wt[:, ab, k, :], hT[:, k, 0:W], start=k == 0, stop=k == DT - 1)
                            last.then_inc(ps_full[b], 1)
                for b in range(4):
                    use["up", l, f, b] = (b, base[b] + 1)
                    bank_uses[b] += FT // 2
                for c in range(c0, c0 + FT):
                    released[c] = (2 * ((c - c0) % 2) + 1, base[2 * ((c - c0) % 2) + 1] + 1 + (c - c0) // 2)
                for b in (1, 3):
                    pe.wait_ge(ps_free[b], bank_uses[b])
                c0 = chunk_at[l, f"down{f}"]
                base = list(bank_uses)
                with pe.Fori(0, DT // 2) as i:
                    for s in range(2):
                        c = c0 + s
                        pe.wait_ge(landed[c % 2], i * 16 + 16 * (c // 2 + 1))
                        wt = ring[:, c % 2, 0:DOWN_CHUNK].rearrange("p (k n) -> p k n", n=P)
                        b = 4 + s
                        pe.wait_ge(ps_free[b], i + base[b])
                        for k in range(FT):
                            last = mm(ps[b][:, 0:W], wt[:, k, :], g_ff[:, k, 0:W], start=k == 0, stop=k == FT - 1)
                        last.then_inc(ps_full[b], 1)
                for d in range(DT):
                    use["down", l, f, d] = (4 + d % 2, base[4 + d % 2] + 1 + d // 2)
                    released[c0 + d] = use["down", l, f, d]
                for b in (4, 5):
                    bank_uses[b] += DT // 2

            def project(l, c, kind, j, W):
                wt = weights(c)[:, 0:PROJ_CHUNK].rearrange("p (k n) -> p k n", k=DT)
                b = bank((kind, l, j))
                for k in range(DT):
                    last = mm(ps[b][:, 0:W], wt[:, k, (j % 2) * P:(j % 2 + 1) * P], hT[:, k, 0:W],
                              start=k == 0, stop=k == DT - 1)
                last.then_inc(ps_full[b], 1)
                used(c, (kind, l, j))

            def level(l, n):
                pair, li = n // len(LEVELS), n % len(LEVELS)
                buf = lev[n % 3]
                (weighted if li else diffs).wait(pe, (l, n))
                for hh in range(2):
                    b = bank(("lev", l, n, hh))
                    for c in range(out_w[l] // P):
                        cols = slice(c * P, (c + 1) * P)
                        rhs = q[:, 2 * pair + hh, cols] if li == 0 else buf[:, 0, hh, cols]
                        last = mm(ps[b][:, cols], buf[:, 1, hh, cols], rhs, start=True, stop=True)
                    last.then_inc(ps_full[b], 1)

            def mixer_in(l):
                W = out_w[l]
                c = chunk_at[l, "proj"]
                pe.wait_ge(tables_in, 32)
                h_ready.wait(pe, (l, 1, DT - 1))
                h_ctx_ready.wait(pe, (l, 1, DT - 1))
                for kind, width in (("zf", T), ("zb", T), ("q", W)):
                    for j in range(4):
                        project(l, c + j // 2, kind, j, width)
                    c += 2
                for half in range(2):
                    wt = weights(c)[:, 0:PROJ_CHUNK].rearrange("p (k n) -> p k n", k=DT)
                    for t in range(CH):
                        b = bank(("v", l, half, t))
                        for k in range(DT):
                            last = mm(ps[b][:, 0:256], hT[:, k, t * P:(t + 1) * P], wt[:, k, :],
                                      start=k == 0, stop=k == DT - 1)
                        last.then_inc(ps_full[b], 1)
                    used(c, ("v", l, half, CH - 1))
                    c += 1
                for j in range(4):
                    project(l, c + j // 2, "g", j, W)
                c += 2
                for n in range(NLEV):
                    if n < 12:
                        project(l, c + n // 2, "hy", n, W)
                    elif n < 14:
                        project(l, c + 6, "qa", n - 12, W)
                    else:
                        kc = chunk_at[l, "kvkr"]
                        wt = weights(kc)[:, 0:KVKR_CHUNK].rearrange("p (k n) -> p k n", k=DT)
                        lo, m = ((0, P), (P, ROPE))[n - 14]
                        b = bank(("kvkr", l, n - 14))
                        for k in range(DT):
                            last = mm(ps[b][0:m, 0:T], wt[:, k, lo:lo + m], hT[:, k, 0:T], start=k == 0, stop=k == DT - 1)
                        last.then_inc(ps_full[b], 1)
                        used(kc, ("kvkr", l, n - 14))
                    if n in MLP_AT:
                        i = MLP_AT.index(n)
                        b = bank(("mlp", l, i))
                        if i:
                            hidden.wait(pe, (l, i - 1))
                        k = EMB if i == 0 else FH
                        mm(ps[b][0:FH, 0:S], sm(l, ("w1", "w2", "w3")[i], 0, FH, k), emb if i == 0 else hid,
                           start=True, stop=True).then_inc(ps_full[b], 1)
                    level(l, n)

            def hgrn_out(l):
                W = out_w[l]
                seq = ((2, 3, 0), (3, 2, 1))
                for dr in range(2):
                    k_decayed.wait(pe, (l, dr))
                    for j, c in enumerate(seq[dr]):
                        b = bank(("kT", l, dr, j))
                        for h in range(H):
                            last = nc.tensor.transpose(ps[b][:, h * P:(h + 1) * P], kd[dr][:, h, c * P:(c + 1) * P], ident)
                        last.then_inc(ps_full[b], 1)
                for j in range(3):
                    for dr in range(2):
                        taken(("kT", l, dr, j))
                        c = seq[dr][j]
                        b = bank(("st", l, j, dr))
                        for h in range(H):
                            cols = slice(h * P, (h + 1) * P)
                            last = mm(ps[b][:, cols], kdT[dr][:, j, cols], val[:, c, cols], start=True, stop=True)
                        last.then_inc(ps_full[b], 1)
                q_decayed.wait(pe, (l, 1))
                taken(("st", l, 2, 1))
                before = ({3: 0, 0: 1, 1: 2}, {2: 0, 1: 1, 0: 2})
                for h in range(H):
                    b = bank(("o", l, h))
                    hc = slice(h * P, (h + 1) * P)
                    for c in range(W // P):
                        cols = slice(c * P, (c + 1) * P)
                        terms = [(val[:, c, hc], attn[:, h, c, :])]
                        for dr in range(2):
                            if c in before[dr]:
                                terms.append((state[dr][:, before[dr][c], hc], bd[dr][:, h, cols]))
                        for i, (a, r) in enumerate(terms):
                            last = mm(ps[b][:, cols], a, r, start=i == 0, stop=i == len(terms) - 1)
                    last.then_inc(ps_full[b], 1)
                for h in range(H):
                    taken(("o", l, h))
                    b = bank(("ostat", l, h))
                    mm(ps[b][:, 0:W], ones[128][:, :], o_sq[:, h, 0:W], start=True, stop=True).then_inc(ps_full[b], 1)

            def hyena(l):
                W = out_w[l]
                hidden.wait(pe, (l, 2))
                pe.wait_ge(hy_in, 32 * (l + 1))
                for t in range(2):
                    for cc in range(4):
                        b = bank(("tap", l, t, cc))
                        mm(ps[b][:, :], hid[:, t * P:(t + 1) * P], w4[:, cc * HYW:(cc + 1) * HYW],
                           start=True, stop=True).then_inc(ps_full[b], 1)
                taps_ready.wait(pe, l)
                for o in range(2):
                    for f in range(2):
                        for part in range(2):
                            b = bank(("kf", l, o, f, part))
                            for t in range(2):
                                last = mm(ps[b][:, :], dft[:, part, t, f * P:(f + 1) * P], even_odd[:, part, t, o, :],
                                          start=t == 0, stop=t == 1)
                            last.then_inc(ps_full[b], 1)
                taps_abs.wait(pe, l)
                b = bank(("l1", l))
                for o in range(2):
                    for ct in range(CT):
                        for i in range(4):
                            t, dr = i // 2, i % 2
                            col = o * CT + ct
                            last = mm(ps[b][:, col:col + 1], taps[:, t, 2 * dr + o, ct * P:(ct + 1) * P], ones[1][:, 0:1],
                                      start=i == 0, stop=i == 3)
                last.then_inc(ps_full[b], 1)
                for o in range(2):
                    conv_done.wait(pe, (l, 11))
                    for t in range(W // P):
                        if o:
                            z_done.wait(pe, (l, 0, t // 2, CT // 2 - 1))
                        b = bank(("zt", l, o, t))
                        for ct in range(CT):
                            last = nc.tensor.transpose(ps[b][:, ct * P:(ct + 1) * P], yb[:, ct, t * P:(t + 1) * P], ident)
                        last.then_inc(ps_full[b], 1)
                    for st in range(W // S):
                        taken(("zt", l, o, 2 * st + 1))
                        for f in range(2):
                            for part in range(2):
                                b = bank(("fw", l, o, st, f, part))
                                for t in range(2):
                                    last = mm(ps[b][:, :], dft[:, part, t, f * P:(f + 1) * P], zt[:, 2 * st + t, :],
                                              start=t == 0, stop=t == 1)
                                last.then_inc(ps_full[b], 1)
                    for st in range(W // S):
                        spect.wait(pe, (l, o, st, 1))
                        for cp in range(CT // 2):
                            b = bank(("inv", l, o, st, cp))
                            for cc in range(2):
                                ct = 2 * cp + cc
                                for i in range(4):
                                    f, part = i // 2, i % 2
                                    last = mm(ps[b][:, cc * S:(cc + 1) * S], spec_y[st][:, f, part, ct * P:(ct + 1) * P],
                                              dft[:, 2 + part, f, :], start=i == 0, stop=i == 3)
                            last.then_inc(ps_full[b], 1)

            def mla(l):
                W = out_w[l]
                for j, (n_t, key) in enumerate(((2, 256), (1, 128), (1, 64))):
                    m_squared.wait(pe, (l, 0, j))
                    b = bank(("ms", l, 0, j))
                    width, p = (W, P) if j == 0 else (T, P if j == 1 else ROPE)
                    for i in range(n_t):
                        src = m_sq[0:p, (0, 2, 3)[j] + i, 0:width]
                        last = mm(ps[b][0:p, 0:width], ones[key][0:p, 0:p], src, start=i == 0, stop=i == n_t - 1)
                    last.then_inc(ps_full[b], 1)
                mc = chunk_at[l, "mla"]
                wt = weights(mc)
                uq = wt[:, 0:1536].rearrange("p (k n) -> p k n", k=2)
                ukv = wt[:, 1536:2560].rearrange("p (h n) -> p h n", h=H)
                m_normed.wait(pe, (l, 0, 1))
                for t in range(CH):
                    b = bank(("vv", l, t))
                    mm(ps[b][:, :].rearrange("p (h n) -> p h n", h=H), lora[:, 2, t * P:(t + 1) * P], ukv[:, :, P:2 * P],
                       start=True, stop=True).then_inc(ps_full[b], 1)
                def products(bt):
                    p = ROPE if bt == 2 else P
                    for h in range(H):
                        b = bank(("mp", l, bt, h))
                        if bt == 3:
                            last = mm(ps[b][:, 0:T], ukv[:, h, 0:P], lora[:, 2, :], start=True, stop=True)
                        else:
                            lo = h * QK + (P if bt == 2 else 0)
                            for k in range(2):
                                last = mm(ps[b][0:p, 0:W], uq[:, k, lo:lo + p], lora[:, k, 0:W], start=k == 0, stop=k == 1)
                        last.then_inc(ps_full[b], 1)

                def sums(bt):
                    p = ROPE if bt == 2 else P
                    width = T if bt == 3 else W
                    for h in range(H):
                        m_squared.wait(pe, (l, bt, h))
                        b = bank(("ms", l, bt, h))
                        mm(ps[b][0:p, 0:width], ones[64 if bt == 2 else 128][0:p, 0:p], m_sq[0:p, h, 0:width],
                           start=True, stop=True).then_inc(ps_full[b], 1)

                products(1)
                products(2)
                sums(1)
                products(3)
                used(mc, ("mp", l, 3, H - 1))
                sums(2)
                sums(3)
                for i in range(5):
                    m_normed.wait(pe, (l, 2, i) if i < 4 else (l, 0, 2))
                    b = bank(("rope", l, i))
                    src = qr[:, i, 0:S] if i < 4 else kr[:, 0:S]
                    mm(ps[b][0:ROPE, 0:S], perm, src, start=True, stop=True).then_inc(ps_full[b], 1)
                m_normed.wait(pe, (l, 3, H - 1))
                roped.wait(pe, (l, 4))
                taken(("vv", l, CH - 1))
                n = len(tiles[l])
                for i in range(n + 3):
                    if i < n:
                        qt, h = tiles[l][i]
                        k0 = 0 if qt < 2 else S
                        b = bank(("sc", l, i))
                        cols = slice(qt * P, (qt + 1) * P)
                        mm(ps[b][:, 0:T - k0], qn[:, h, cols], kn[:, h, k0:T], start=True, stop=False)
                        mm(ps[b][:, 0:T - k0], qr[:, h, cols], kr[:, k0:T], start=False, stop=True).then_inc(ps_full[b], 1)
                    if 2 <= i < n + 2:
                        qt, h = tiles[l][i - 2]
                        nk = CH if qt < 2 else 2
                        prob_ready.wait(pe, (l, i - 2))
                        b = bank(("pt", l, i - 2))
                        for kt in range(nk):
                            last = nc.tensor.transpose(ps[b][:, kt * P:(kt + 1) * P],
                                                       prob[:, (i - 2) % 4, kt * P:(kt + 1) * P], ident)
                        last.then_inc(ps_full[b], 1)
                    if i >= 3:
                        qt, h = tiles[l][i - 3]
                        nk = CH if qt < 2 else 2
                        taken(("pt", l, i - 3))
                        b = bank(("av", l, i - 3))
                        for kt in range(nk):
                            last = mm(ps[b][:, 0:P], vv[:, CH - nk + kt, h * P:(h + 1) * P], probT[:, (i - 3) % 2, kt, :],
                                      start=kt == 0, stop=kt == nk - 1)
                        last.then_inc(ps_full[b], 1)
                taken(("av", l, n - 1))

            def merge(l):
                W = out_w[l]
                ya_done.wait(pe, (l, H - 1))
                z_done.wait(pe, (l, 1, out_w[l] // S - 1, CT // 2 - 1))
                for br, y in enumerate((ya, yb, yc)):
                    for qd in range(4):
                        c = chunk_at[l, "merge"] + 4 * br + qd
                        wt = weights(c)
                        wg = wt[:, 0:2048].rearrange("p (k n) -> p k n", k=DT)
                        wb = wt[:, 2048:3072].rearrange("p (k n) -> p k n", k=4)
                        for dd in range(2):
                            d = 2 * qd + dd
                            cols = slice(dd * P, (dd + 1) * P)
                            b = bank(("gate", l, br, d))
                            for k in range(DT):
                                last = mm(ps[b][:, 0:W], wg[:, k, cols], hT[:, k, 0:W], start=k == 0, stop=k == DT - 1)
                            last.then_inc(ps_full[b], 1)
                            b = bank(("br", l, br, d))
                            for k in range(4):
                                last = mm(ps[b][:, 0:W], wb[:, k, cols], y[:, k, 0:W], start=k == 0, stop=k == 3)
                            last.then_inc(ps_full[b], 1)
                        used(c, ("br", l, br, 2 * qd + 1))
                mixed.wait(pe, (l, DT - 1))
                for d in range(DT):
                    c = chunk_at[l, "out"] + d // 2
                    wt = weights(c)[:, 0:PROJ_CHUNK].rearrange("p (k n) -> p k n", k=DT)
                    b = bank(("out", l, d))
                    for k in range(DT):
                        last = mm(ps[b][:, 0:W], wt[:, k, (d % 2) * P:(d % 2 + 1) * P], mix[:, k, 0:W],
                                  start=k == 0, stop=k == DT - 1)
                    last.then_inc(ps_full[b], 1)
                    used(c, ("out", l, d))

            warm()
            for l in range(L):
                norm(l, 0)
                ffn(l, 0)
                norm(l, 1)
                mixer_in(l)
                hgrn_out(l)
                hyena(l)
                mla(l)
                merge(l)
                norm(l, 2)
                ffn(l, 1)

        def full(eng, key):
            b, n = use[key]
            eng.wait_ge(ps_full[b], n)
            return ps[b]

        def freed(key):
            b, n = use[key]
            return ps_free[b], n

        def x_ready(l, w):
            if w == 0:
                return [(x_in, 32)] * DT if l == 0 else [freed(("down", l - 1, 1, d)) for d in range(DT)]
            return [freed(("down", l, 0, d) if w == 1 else ("out", l, d)) for d in range(DT)]

        @block.sync
        def _(sp):
            def load_c():
                for s, name in enumerate(("c", "c_ctx")):
                    sp.dma_start(c_row[:, s, :], dram[name].partition_broadcast(P)).then_inc(c_in, 16)

            load_c()
            sp.dma_start(small[:, :, :], dram["small"]).then_inc(params_in, 16)
            sp.dma_start(logits[:, :, :, :], dram["logits"]).then_inc(params_in, 16)
            for s in range(4):
                lo, n = s * FIRST // 4, FIRST // 4
                sp.dma_start(ada_first[:, lo:lo + n, :], dram["ada"][0, lo:lo + n, :, :].rearrange("n p d -> p n d"))\
                    .then_inc(ada_first_in[s], 16)
            for c in range(2):
                sp.dma_start(xT[:, 4 * c:4 * c + 4, :], dram["xT"][:, 4 * c:4 * c + 4, :]).then_inc(x_in, 16)
            sp.dma_start(fixed[:, :], dram["fixed"]).then_inc(tables_in, 16)
            sp.dma_start(masks[:, :, :], dram["masks"]).then_inc(tables_in, 16)
            source = {"proj": "proj", "kvkr": "kvkr", "mla": "mla", "merge": "merge", "out": "wout",
                      "up0": "up0", "up1": "up1", "down0": "down0", "down1": "down1"}

            def load(c):
                l, key, j = order[c]
                src = dram[source[key]][l, j, :, :]
                if c >= 2:
                    b, n = released[c - 2]
                    sp.wait_ge(ps_full[b], n)
                sp.dma_start(ring[:, c % 2, 0:src.shape[1]], src).then_inc(landed[c % 2], 16)

            def load_loop(c0, n):
                l, key, _ = order[c0]
                f = int(key[-1])
                plan = ADA_PLAN.get((l, f)) if key[:2] == "up" else None
                f = int(f)
                turns_before = [f * (FT // 2 + (ADA_REST[0, 0] > 3 * g)) for g in range(2)]
                load(c0)
                load(c0 + 1)

                def load_ada(g, tile, count):
                    src = dram["ada"][ADA_PLAN[l, f][0], tile:tile + count, :, :]
                    sp.dma_start(ada_buf[g][:, 0:count, :], src.rearrange("n p d -> p n d")).then_inc(ada_landed[g], 16)

                if plan:
                    if f:
                        sp.wait_ge(*freed(("out", l, DT - 1)))
                        load_c()
                    for g in range(2):
                        load_ada(g, plan[1] + g * plan[2][0], plan[2][g])
                if key[:4] == "down" and (l, f) in ADA_PLAN:
                    at = MOD_TILES - ADA_REST[l, f]
                    for g in range(2):
                        count = min(3, MOD_TILES - at)
                        if count > 0:
                            sp.wait_ge(ada_used[g], turns_before[g] + FT // 2)
                            load_ada(g, at, count)
                            at += count
                with sp.Fori(1, n // 2) as i:
                    for s in range(2):
                        b, m = released[c0 + s]
                        sp.wait_ge(ps_full[b], i + (m - 1))
                        src = dram[source[key]][l, bass.ds(i * 2 + s, 1), :, :].rearrange("o p n -> p (o n)")
                        sp.dma_start(ring[:, (c0 + s) % 2, 0:src.shape[1]], src).then_inc(landed[(c0 + s) % 2], 16)
                        if plan:
                            ada_l, first, groups = plan
                            sp.wait_ge(ada_used[s], i + turns_before[s])
                            src = dram["ada"][ada_l, bass.ds(i * sum(groups) + (first + s * groups[0]), groups[s]), :, :]
                            sp.dma_start(ada_buf[s][:, 0:groups[s], :], src.rearrange("n p d -> p n d"))\
                                .then_inc(ada_landed[s], 16)

            for l in range(L):
                for f in range(2):
                    load_loop(chunk_at[l, f"up{f}"], FT)
                    load_loop(chunk_at[l, f"down{f}"], DT)
                    if f == 1:
                        continue
                    for c in range(chunk_at[l, "proj"], chunk_at[l, "mla"]):
                        load(c)
                    full(sp, ("o", l, H - 1))
                    sp.dma_start(hy_tab[:, :], dram["hy_tab"]).then_inc(hy_in, 16)
                    sp.dma_start(w4, dram["w4"][l, :, :]).then_inc(hy_in, 16)
                    for c in range(chunk_at[l, "mla"], chunk_at[l, "up1"]):
                        load(c)
            for d in range(DT):
                sp.wait_ge(*freed(("down", L - 1, 1, d)))
                sp.dma_start(out[:, d, :], xT[:, d, 0:S]).then_inc(y_out, 16)
            sp.wait_ge(y_out, 16 * DT)

        @block.scalar
        def _(act):
            do = Steps(act, scalar_steps)
            A = nc.scalar.activation

            def norm(l, w):
                W = widths[l, w]
                ready = x_ready(l, w)
                for d in range(DT):
                    act.wait_ge(*ready[d])
                    do(A(hT[:, d, 0:W], xT[:, d, 0:W], ACT.Square), squared.of((l, w, d)))
                src = full(act, ("stat", l, w))
                do(A(root[:, 0:W], src[:, 0:W], ACT.Sqrt, bias=eps_t[:, :]), freed(("stat", l, w)))
                for d in range(DT):
                    scaled.wait(act, (l, w, d))
                    do(A(hT[:, d, 0:S], hT[:, d, 0:S], ACT.Identity, scale=gain_s[:, l, w, d, 0:1],
                         bias=mod[:, l, 3 * w * DT + d, 0:1]), h_ready.of((l, w, d)))

            def ffn(l, f):
                W = widths[l, 2 * f]
                with act.Fori(0, FT // 2) as i:
                    for s in range(2):
                        na, nb = use["up", l, f, 2 * s][1], use["up", l, f, 2 * s + 1][1]
                        act.wait_ge(ps_full[2 * s], i + na)
                        act.wait_ge(ps_free[2 * s + 1], i + (nb - 1))
                        A(silu_ff[:, s, 0:W], ps[2 * s][:, 0:W], ACT.Silu).then_inc(ps_free[2 * s], 1)

            def take(key, dst, src_cols, func=ACT.Copy, p=P):
                src = full(act, key)
                do(A(dst, src[0:p, 0:src_cols], func), freed(key))

            def mixer_in(l):
                W = out_w[l]
                for dr, kind in enumerate(("zf", "zb")):
                    for j in range(4):
                        take((kind, l, j), kd[dr][:, j, :], T, ACT.Sigmoid)
                for j in range(4):
                    take(("q", l, j), q[:, j, 0:W], W, ACT.Silu)
                for half in range(2):
                    for t in range(CH):
                        take(("v", l, half, t), val[:, t, half * 256:(half + 1) * 256], 256)
                for n in range(8):
                    f_split.wait(act, (l, n))
                    do(A(bd[n // 4][:, n % 4, :], bd[n // 4][:, n % 4, :], ACT.Ln))
                    do(A(split[:, n // 4, n % 4, :], split[:, n // 4, n % 4, :], ACT.Ln), logged.of((l, n)))
                for j in range(4):
                    take(("g", l, j), ya[:, j, 0:W], W, ACT.Silu)
                for n in range(NLEV):
                    if n % len(LEVELS):
                        diffs.wait(act, (l, n))
                        do(A(lev[n % 3][:, :, :, 0:W], lev[n % 3][:, :, :, 0:W], ACT.Exp), decays.of((l, n)))
                    if n < 12:
                        src = full(act, ("hy", l, n))
                        if n >= 2:
                            conv_done.wait(act, (l, n - 2))
                        elif l:
                            conv_done.wait(act, (l - 1, 10 + n))
                        for st in range(W // S):
                            do(A(upad[:, n % 2, st, 1:S + 1], src[:, st * S:(st + 1) * S], ACT.Copy))
                        do(A(uc[:, n, 0:W], src[:, 0:W], ACT.Identity, scale=sm(l, "conv_w", 12 + n),
                             bias=sm(l, "conv_b", n)), freed(("hy", l, n)))
                    elif n < 14:
                        take(("qa", l, n - 12), raw[:, n - 12, 0:W], W)
                    else:
                        p = P if n == 14 else ROPE
                        take(("kvkr", l, n - 14), raw[0:p, n - 12, :], T, p=p)
                    if n in MLP_AT:
                        phase.wait(act, (l, MLP_AT.index(n)))
                        do(A(hid, arg, ACT.Sin), hidden.of((l, MLP_AT.index(n))))

            def hgrn_out(l):
                W = out_w[l]
                for dr in range(2):
                    tail_diff.wait(act, (l, dr))
                    do(A(tail[dr], tail[dr], ACT.Exp))
                    do(A(bd[dr], bd[dr], ACT.Exp), tail_exp.of((l, dr)))
                for dr in range(2):
                    for j in range(3):
                        take(("kT", l, dr, j), kdT[dr][:, j, :], 512)
                for h in range(H):
                    src = full(act, ("o", l, h))
                    do(A(o_raw[:, h, 0:W], src[:, 0:W], ACT.Copy))
                    do(A(o_sq[:, h, 0:W], src[:, 0:W], ACT.Square), freed(("o", l, h)))
                for h in range(H):
                    src = full(act, ("ostat", l, h))
                    do(A(o_root[:, h, 0:W], src[:, 0:W], ACT.Sqrt, bias=eps_t[:, :]), freed(("ostat", l, h)))

            def hyena(l):
                W = out_w[l]
                taps_ready.wait(act, l)
                do(A(taps, taps, ACT.Abs), taps_abs.of(l))
                for o in range(2):
                    for f in range(2):
                        for part in range(2):
                            take(("kf", l, o, f, part), spectrum[:, o, f, part, :], HYW)
                for o in range(2):
                    for t in range(W // P):
                        take(("zt", l, o, t), zt[:, t, :], HYW)

            def mla(l):
                W = out_w[l]
                z_done.wait(act, (l, 1, out_w[l] // S - 1, CT // 2 - 1))
                for j, (at, n, width, p) in enumerate(((0, 2, W, P), (2, 1, T, P), (3, 1, T, ROPE))):
                    for i in range(n):
                        ins = A(m_sq[0:p, at + i, 0:width], raw[0:p, at + i, 0:width], ACT.Square)
                        do(ins, m_squared.of((l, 0, j)) if i == n - 1 else None)
                for j, (width, p) in enumerate(((W, P), (T, P), (T, ROPE))):
                    src = full(act, ("ms", l, 0, j))
                    do(A(m_root[0:p, j, 0:width], src[0:p, 0:width], ACT.Sqrt, bias=eps_t[0:p, :]), freed(("ms", l, 0, j)))
                for t in range(CH):
                    take(("vv", l, t), vv[:, t, :], 512)
                for bt in range(1, 4):
                    p = ROPE if bt == 2 else P
                    width = T if bt == 3 else W
                    for h in range(H):
                        src = full(act, ("mp", l, bt, h))
                        if bt > 1:
                            m_normed.wait(act, (l, bt - 1, h))
                        elif h == 0:
                            m_normed.wait(act, (l, 0, 2))
                        do(A(m_sq[0:p, h, 0:width], src[0:p, 0:width], ACT.Square), m_squared.of((l, bt, h)))
                        do(A(m_raw[0:p, h, 0:width], src[0:p, 0:width], ACT.Copy), freed(("mp", l, bt, h)))
                    for h in range(H):
                        src = full(act, ("ms", l, bt, h))
                        do(A(m_root[0:p, h, 0:width], src[0:p, 0:width], ACT.Sqrt, bias=eps_t[0:p, :]),
                           freed(("ms", l, bt, h)))
                n = len(tiles[l])
                for i in range(n + 3):
                    if i < n:
                        qt, h = tiles[l][i]
                        nk = T if qt < 2 else S
                        src = full(act, ("sc", l, i))
                        row_max.wait(act, (l, i))
                        if i >= 4:
                            full(act, ("pt", l, i - 4))
                        do(A(prob[:, i % 4, 0:nk], src[:, 0:nk], ACT.Exp, bias=mxt[:, i % 4, 1:2], scale=SCALE,
                             accum_out=mxt[:, i % 4, 2:3]), exped.of((l, i)))
                    if 2 <= i < n + 2:
                        qt, h = tiles[l][i - 2]
                        nk = T if qt < 2 else S
                        if i >= 4:
                            full(act, ("av", l, i - 4))
                        take(("pt", l, i - 2), probT[:, i % 2, 0:nk // P, :].rearrange("p k q -> p (k q)"), nk)
                    if i >= 3:
                        qt, h = tiles[l][i - 3]
                        take(("av", l, i - 3), yc[:, h, qt * P:(qt + 1) * P], P)

            def merge(l):
                W = out_w[l]
                for br in range(3):
                    for d in range(DT):
                        n = br * DT + d
                        if n >= 2:
                            act.wait_ge(*freed(("br", l, (n - 2) // DT, (n - 2) % DT)))
                        take(("gate", l, br, d), gate_t[:, n % 2, 0:W], W, ACT.Sigmoid)

            def silu_c(n):
                act.wait_ge(c_in, 32 * (n + 1))
                do(A(c_row, c_row, ACT.Silu), c_silu.of(n))

            silu_c(0)
            act.wait_ge(params_in, 16 * 2)
            consts.wait(act, 0)
            lb_max.wait(act, 0)
            do(A(lb_e[:, :, :, :], lb_e[:, :, :, :], ACT.Exp), lb_exp.of(0))
            for l in range(L):
                norm(l, 0)
                ffn(l, 0)
                norm(l, 1)
                mixer_in(l)
                hgrn_out(l)
                hyena(l)
                mla(l)
                merge(l)
                norm(l, 2)
                if (l, 1) in ADA_PLAN:
                    silu_c(1)
                ffn(l, 1)

        @block.vector
        def _(dve):
            do = Steps(dve, vector_steps)
            tt, ts, stt = nc.vector.tensor_tensor, nc.vector.tensor_scalar, nc.vector.scalar_tensor_tensor

            def then(ins, event=None):
                do(ins, event)
                do.settle()

            def setup():
                for n, t in ones.items():
                    do(nc.vector.memset(t[:, :], 1.0 / n))
                do(nc.vector.memset(upad, 0.0))
                do(nc.vector.memset(eps_t[:, :], EPS), consts.of(0))
                for b in range(8):
                    dve.wait_ge(ps_full[b], 1)
                    do(nc.vector.tensor_copy(elast[:, 0, 0:1], ps[b][:, 0:1]), (ps_free[b], 1))
                    do.settle()
                dve.wait_ge(params_in, 16 * 2)
                for l in range(L):
                    then(tt(lb_t[:, :, 0, :], logits[:, :, 0, :], logits[:, :, 1, :], ALU.max))
                for l in range(L):
                    do(tt(lb_e[:, :, l, :], logits[:, :, l, :], lb_t[:, :, 0, :], ALU.subtract),
                       lb_max.of(0) if l == L - 1 else None)
                lb_exp.wait(dve, 0)
                then(tt(lb_t[:, :, 0, :], lb_e[:, :, 0, :], lb_e[:, :, 1, :], ALU.add))
                then(nc.vector.reciprocal(lb_t[:, :, 1, :], lb_t[:, :, 0, :]))
                for l in range(L):
                    then(tt(lb_e[:, :, l, :], lb_e[:, :, l, :], lb_t[:, :, 1, :], ALU.mult))
                then(nc.vector.tensor_copy(lb_t[:, :, 0, :], lb_e[:, :, 0, :]))
                for l in range(L):
                    if l:
                        then(tt(lb_t[:, :, 0, :], lb_t[:, :, 0, :], lb_e[:, :, l, :], ALU.add))
                    then(tt(lb[:, :, l, :], lb_t[:, :, 0, :], lb_e[:, :, 0, :], ALU.subtract))
                    then(ts(lb1[:, :, l, :], lb[:, :, l, :], -1.0, 1.0, ALU.mult, ALU.add))

            def dots(src, acc, n, event):
                for j in range(n):
                    for s in range(2):
                        ins = nc.vector.tensor_tensor_reduce(
                            out=src[:, j, :] if s else ada_prod[:, j, :], in0=src[:, j, :], in1=c_row[:, s, :], scale=1.0, scalar=0.0, op0=ALU.mult,
                            op1=ALU.add, accum_out=acc[:, j, s:s + 1])
                        if (j, s) == (n - 1, 1) and event:
                            ins.then_inc(*event)
                return ins

            def ada_head():
                c_silu.wait(dve, 0)
                for s in range(4):
                    lo = s * FIRST // 4
                    dve.wait_ge(ada_first_in[s], 16)
                    do(dots(ada_first[:, lo:lo + FIRST // 4, :], mod[:, 0, lo:lo + FIRST // 4, :], FIRST // 4, None))
                    do.settle()
                add_bias(0, 0, FIRST)
                gains(0, 0)

            def add_bias(l, lo, n):
                bias = sm(l, "ada_b", lo, n).unsqueeze(2).broadcast_to([P, n, 2])
                then(tt(mod[:, l, lo:lo + n, :], mod[:, l, lo:lo + n, :], bias, ALU.add))

            def gains(l, w):
                name = ("ffn1_norm", "mix_norm", "ffn2_norm")[w]
                at = 3 * w * DT
                gain = sm(l, name, 0, DT).unsqueeze(2).broadcast_to([P, DT, 2])
                then(stt(gain_s[:, l, w, :, :], mod[:, l, at + DT:at + 2 * DT, :], 1.0, gain, ALU.add, ALU.mult))

            def gates(l, w):
                at = 3 * w * DT
                then(ts(gate_s[:, l, w, :, :], mod[:, l, at + 2 * DT:at + 3 * DT, :], 1.0 if w == 1 else 0.5, None, ALU.mult))

            def norm(l, w):
                W = widths[l, w]
                dve.wait_ge(*freed(("stat", l, w)))
                then(nc.vector.reciprocal(root[:, 0:W], root[:, 0:W]))
                if (l, w) == (0, 0):
                    dve.wait_ge(x_in, 32)
                for d in range(DT):
                    do(tt(hT[:, d, 0:W], xT[:, d, 0:W], root[:, 0:W], ALU.mult), scaled.of((l, w, d)))
                if W == T:
                    do.settle()
                    for d in range(DT):
                        do(ts(hT[:, d, S:T], hT[:, d, S:T], gain_s[:, l, w, d, 1:2], mod[:, l, 3 * w * DT + d, 1:2],
                              ALU.mult, ALU.add), h_ctx_ready.of((l, w, d)))

            def add_to_x(l, w, key, d, W):
                src = full(dve, key)
                for st in range(W // S):
                    cols = slice(st * S, (st + 1) * S)
                    do(stt(xT[:, d, cols], src[:, cols], gate_s[:, l, w, d, st:st + 1], xT[:, d, cols], ALU.mult, ALU.add),
                       freed(key) if st == W // S - 1 else None)

            def ffn(l, f):
                W = widths[l, 2 * f]
                plan = ADA_PLAN.get((l, f))
                turns_before = [f * (FT // 2 + (ADA_REST[0, 0] > 3 * g)) for g in range(2)]
                if plan:
                    c_silu.wait(dve, f)
                with dve.Fori(0, FT // 2) as i:
                    for s in range(2):
                        na, nb = use["up", l, f, 2 * s][1], use["up", l, f, 2 * s + 1][1]
                        dve.wait_ge(ps_free[2 * s], i + na)
                        dve.wait_ge(ps_full[2 * s + 1], i + nb)
                        tt(g_ff[:, bass.ds(i * 2 + s, 1), 0:W].rearrange("p o t -> p (o t)"), silu_ff[:, s, 0:W],
                           ps[2 * s + 1][:, 0:W], ALU.mult).then_inc(ps_free[2 * s + 1], 1)
                        if plan:
                            ada_l, first, groups = plan
                            dve.wait_ge(ada_landed[s], i * 16 + 16 * (turns_before[s] + 1))
                            dots(ada_buf[s], ada_acc[:, s, :, :], groups[s], (ada_used[s], 1))
                            dve.wait_ge(ada_used[s], i + (turns_before[s] + 1))
                            at = i * sum(groups) + (first + s * groups[0])
                            nc.vector.tensor_copy(mod[:, ada_l, bass.ds(at, groups[s]), :], ada_acc[:, s, 0:groups[s], :])\
                                .then_inc(mod_written, 1)
                if plan:
                    ada_l, first, _ = plan
                    at = MOD_TILES - ADA_REST[l, f]
                    for g in range(2):
                        count = min(3, MOD_TILES - at)
                        if count > 0:
                            dve.wait_ge(ada_landed[g], 16 * (turns_before[g] + FT // 2 + 1))
                            do(dots(ada_buf[g], mod[:, ada_l, at:at + count, :], count, None), (ada_used[g], turns_before[g] + FT // 2 + 1))
                            do.settle()
                            at += count
                    dve.wait_ge(mod_written, FT * (f + 1))
                    add_bias(ada_l, first, MOD_TILES - first)
                    for w in range(3):
                        if (ada_l, w) != (0, 0):
                            gains(ada_l, w)
                        gates(ada_l, w)
                for d in range(DT):
                    add_to_x(l, 2 * f, ("down", l, f, d), d, W)

            def level_views(a, m):
                v = a.rearrange("p h (n two m) -> p h n two m", two=2, m=m)
                return v[:, :, :, 0, :], v[:, :, :, 1, :]

            def level_diff(l, n):
                W, m, hs = out_w[l], LEVELS[n % len(LEVELS)], slice(2 * (n // len(LEVELS)), 2 * (n // len(LEVELS)) + 2)
                buf = lev[n % 3]
                if m == 0:
                    do(tt(buf[:, 1, :, 0:W], kd[0][:, hs, 0:W], kd[1][:, hs, 0:W], ALU.add), diffs.of((l, n)))
                    return
                f0, f1 = level_views(bd[0][:, hs, 0:W], m)
                g0, g1 = level_views(bd[1][:, hs, 0:W], m)
                q0, q1 = level_views(buf[:, 0, :, 0:W], m)
                k0, k1 = level_views(buf[:, 1, :, 0:W], m)
                rf = f0[:, :, :, m - 1:m].broadcast_to(list(f0.shape))
                rg = g1[:, :, :, 0:1].broadcast_to(list(g1.shape))
                do(tt(q1, f1, rf, ALU.subtract))
                do(tt(k0, rf, f0, ALU.subtract))
                do(tt(q0, g0, rg, ALU.subtract))
                do(tt(k1, rg, g1, ALU.subtract), diffs.of((l, n)))

            def level_weigh(l, n):
                W, m, hs = out_w[l], LEVELS[n % len(LEVELS)], slice(2 * (n // len(LEVELS)), 2 * (n // len(LEVELS)) + 2)
                buf = lev[n % 3]
                if m == 0:
                    return
                decays.wait(dve, (l, n))
                k0, k1 = level_views(buf[:, 1, :, 0:W], m)
                f0, _ = level_views(kd[0][:, hs, 0:W], m)
                _, g1 = level_views(kd[1][:, hs, 0:W], m)
                do(tt(k0, k0, f0, ALU.mult))
                do(tt(k1, k1, g1, ALU.mult))
                do(tt(buf[:, 0, :, 0:W], buf[:, 0, :, 0:W], q[:, hs, 0:W], ALU.mult), weighted.of((l, n)))

            def level_take(l, n):
                nc_, li = out_w[l] // P, n % len(LEVELS)
                do.settle()
                for hh in range(2):
                    h = 2 * (n // len(LEVELS)) + hh
                    key = ("lev", l, n, hh)
                    src = full(dve, key)[:, 0:nc_ * P].rearrange("p (c t) -> p c t", t=P)
                    if li == 0:
                        do(nc.vector.tensor_copy(attn[:, h, 0:nc_, :], src), freed(key))
                    else:
                        mask = masks[:, li:li + 1, :].broadcast_to([P, nc_, P])
                        do(nc.vector.copy_predicated(attn[:, h, 0:nc_, :], mask, src), freed(key))

            def mixer_in(l):
                W = out_w[l]
                dve.wait_ge(tables_in, 32)
                for n in range(8):
                    dr, j = n // 4, n % 4
                    dve.wait_ge(*freed((("zf", "zb")[dr], l, j)))
                    k, b = kd[dr][:, j, :], bd[dr][:, j, :]
                    then(ts(k, k, lb1[:, dr, l, j:j + 1], lb[:, dr, l, j:j + 1], ALU.mult, ALU.add))
                    do(ts(b, k, TINY, None, ALU.max))
                    then(ts(split[:, dr, j, :], k, 1.0 / TINY, 1.0, ALU.mult, ALU.min), f_split.of((l, n)))
                    do(ts(k, k, -1.0, 1.0, ALU.mult, ALU.add))
                for j in range(4):
                    dve.wait_ge(*freed(("q", l, j)))
                    do(ts(q[:, j, 0:W], q[:, j, 0:W], DK ** -0.5, None, ALU.mult))
                for n in range(8):
                    dr, j = n // 4, n % 4
                    logged.wait(dve, (l, n))
                    b = bd[dr][:, j, :]
                    then(tt(b, b, split[:, dr, j, :], ALU.add))
                    for c in range(CH):
                        v = b[:, c * P:(c + 1) * P]
                        if dr:
                            v = v[:, ::-1]
                        do(nc.vector.tensor_tensor_scan(v, ones[1][:, :], v, 0.0, ALU.mult, ALU.add))
                do.settle()
                level_diff(l, 0)
                for n in range(NLEV):
                    if n:
                        level_take(l, n - 1)
                    if n + 1 < NLEV:
                        level_diff(l, n + 1)
                    level_weigh(l, n)
                    if n < 12:
                        dve.wait_ge(*freed(("hy", l, n)))
                        for tap, lo in ((0, 0), (2, 2)):
                            do.settle()
                            for st in range(W // S):
                                cols = slice(st * S, (st + 1) * S)
                                do(stt(uc[:, n, cols], upad[:, n % 2, st, lo:lo + S], sm(l, "conv_w", 12 * tap + n),
                                       uc[:, n, cols], ALU.mult, ALU.add),
                                   conv_done.of((l, n)) if tap and st == W // S - 1 else None)
                    if n in MLP_AT:
                        filter_phase(l, MLP_AT.index(n))
                level_take(l, NLEV - 1)

            def filter_phase(l, i):
                name = ("b1", "b2", "b3")[i]
                src = full(dve, ("mlp", l, i))
                if i:
                    hidden.wait(dve, (l, i - 1))
                then(ts(arg, src[0:FH, 0:S], sm(l, name, p=FH), sm(l, "freq", p=FH), ALU.add, ALU.mult),
                     freed(("mlp", l, i)))
                then(ts(turns, arg, 1.0 / TWO_PI, ROUND, ALU.mult, ALU.add))
                then(ts(turns, turns, ROUND, None, ALU.subtract))
                for part in (PI_A, PI_B, PI_C):
                    then(stt(arg, turns, -part, arg, ALU.mult, ALU.add))
                do(ts(arg, arg, 3.1415925, -3.1415925, ALU.min, ALU.max), phase.of((l, i)))

            def hgrn_out(l):
                W = out_w[l]
                seq = ((2, 3, 0), (3, 2, 1))
                for dr in range(2):
                    at = P - 1 if dr == 0 else 0
                    v = bd[dr].rearrange("p h (c t) -> p (h c) t", t=P)
                    tv = tail[dr].rearrange("p h (c t) -> p (h c) t", t=P)
                    do(tt(tv, v[:, :, at:at + 1].broadcast_to([P, 16, P]), v, ALU.subtract), tail_diff.of((l, dr)))
                for dr in range(2):
                    at = P - 1 if dr == 0 else 0
                    tail_exp.wait(dve, (l, dr))
                    do(tt(kd[dr], kd[dr], tail[dr], ALU.mult), k_decayed.of((l, dr)))
                    v = bd[dr].rearrange("p h (c t) -> p (h c) t", t=P)
                    then(nc.vector.tensor_copy(elast[:, dr, :].unsqueeze(2), v[:, :, at:at + 1]))
                    do(tt(bd[dr][:, :, 0:W], bd[dr][:, :, 0:W], q[:, :, 0:W], ALU.mult), q_decayed.of((l, dr)))
                for j in range(3):
                    for dr in range(2):
                        src = full(dve, ("st", l, j, dr))
                        do.settle()
                        if j == 0:
                            do(nc.vector.tensor_copy(state[dr][:, 0, :], src[:, :]), freed(("st", l, j, dr)))
                        else:
                            for h in range(H):
                                col = h * CH + seq[dr][j]
                                hc = slice(h * P, (h + 1) * P)
                                do(stt(state[dr][:, j, hc], state[dr][:, j - 1, hc], elast[:, dr, col:col + 1], src[:, hc],
                                       ALU.mult, ALU.add), freed(("st", l, j, dr)) if h == H - 1 else None)
                for h in range(H):
                    dve.wait_ge(*freed(("ostat", l, h)))
                    then(nc.vector.reciprocal(o_root[:, h, 0:W], o_root[:, h, 0:W]))
                    then(tt(o_raw[:, h, 0:W], o_raw[:, h, 0:W], o_root[:, h, 0:W], ALU.mult))
                    do(stt(ya[:, h, 0:W], o_raw[:, h, 0:W], sm(l, "hg_out_norm"), ya[:, h, 0:W], ALU.mult, ALU.mult),
                       ya_done.of((l, h)))

            def hyena(l):
                W = out_w[l]
                dve.wait_ge(hy_in, 32 * (l + 1))
                for t in range(2):
                    for cc in range(4):
                        src = full(dve, ("tap", l, t, cc))
                        do(tt(taps[:, t, cc, :], src[:, :], window[:, cc // 2, t, :], ALU.mult), freed(("tap", l, t, cc)))
                do.settle()
                for t in range(2):
                    do(tt(even_odd[:, 0, t, :, :], taps[:, t, 0:2, :], taps[:, t, 2:4, :], ALU.add))
                    do(tt(even_odd[:, 1, t, :, :], taps[:, t, 0:2, :], taps[:, t, 2:4, :], ALU.subtract),
                       taps_ready.of(l) if t else None)
                src = full(dve, ("l1", l))
                then(nc.vector.reciprocal(rnorm[:, :], src[:, 0:8]), freed(("l1", l)))
                then(ts(rnorm[:, :], rnorm[:, :], 2.0 / 512, None, ALU.mult))
                for o in range(2):
                    for st in range(W // S):
                        for f in range(2):
                            if f == 0 and st == 0:
                                dve.wait_ge(*freed(("kf", l, 1, 1, 1)))
                            kp, kq = spectrum[:, o, f, 0, :], spectrum[:, o, f, 1, :]
                            a = full(dve, ("fw", l, o, st, f, 0))
                            do.settle()
                            do(tt(prod[:, 0, :], a[:, :], kp, ALU.mult))
                            do(tt(prod[:, 1, :], a[:, :], kq, ALU.mult), freed(("fw", l, o, st, f, 0)))
                            b = full(dve, ("fw", l, o, st, f, 1))
                            do(tt(prod[:, 2, :], b[:, :], kq, ALU.mult))
                            then(tt(prod[:, 3, :], b[:, :], kp, ALU.mult), freed(("fw", l, o, st, f, 1)))
                            do(tt(spec_y[st][:, f, 0, :], prod[:, 0, :], prod[:, 2, :], ALU.subtract))
                            do(tt(spec_y[st][:, f, 1, :], prod[:, 1, :], prod[:, 3, :], ALU.add), spect.of((l, o, st, f)))
                    do.settle()
                    for ct in range(CT):
                        do(ts(prod[:, ct, 0:W], yb[:, ct, 0:W], sm(l, "skip", o * CT + ct), None, ALU.mult))
                    do.settle()
                    for st in range(W // S):
                        cols = slice(st * S, (st + 1) * S)
                        for cp in range(CT // 2):
                            src = full(dve, ("inv", l, o, st, cp))
                            for cc in range(2):
                                ct = 2 * cp + cc
                                do(stt(prod[:, ct, cols], src[:, cc * S:(cc + 1) * S],
                                       rnorm[:, o * CT + ct:o * CT + ct + 1], prod[:, ct, cols], ALU.mult, ALU.add),
                                   freed(("inv", l, o, st, cp)) if cc else None)
                            do.settle()
                            do(tt(yb[:, 2 * cp:2 * cp + 2, cols], prod[:, 2 * cp:2 * cp + 2, cols],
                                  uc[:, o * CT + 2 * cp:o * CT + 2 * cp + 2, cols], ALU.mult), z_done.of((l, o, st, cp)))

            def mla(l):
                W = out_w[l]
                for j, (n, width, p, name) in enumerate(((2, W, P, "q_a_norm"), (1, T, P, "kv_a_norm"), (1, T, ROPE, "k_rope_norm"))):
                    dve.wait_ge(*freed(("ms", l, 0, j)))
                    r = m_root[0:p, j, 0:width]
                    then(nc.vector.reciprocal(r, r))
                    for i in range(n):
                        dst = kr if j == 2 else lora[:, 2 * j + i, 0:width]
                        do(stt(dst, raw[0:p, (0, 2, 3)[j] + i, 0:width], sm(l, name, i, 1, p), r, ALU.mult, ALU.mult),
                           m_normed.of((l, 0, j)) if i == n - 1 else None)
                for bt, (name, dst) in enumerate((("q_nope_norm", qn), ("q_rope_norm", qr), ("k_nope_norm", kn)), 1):
                    p = ROPE if bt == 2 else P
                    width = T if bt == 3 else W
                    for h in range(H):
                        dve.wait_ge(*freed(("ms", l, bt, h)))
                        r = m_root[0:p, h, 0:width]
                        then(nc.vector.reciprocal(r, r))
                        do(stt(dst[:, h, 0:width], m_raw[0:p, h, 0:width], sm(l, name, 0, 1, p), r, ALU.mult, ALU.mult),
                           m_normed.of((l, bt, h)))
                for i in range(5):
                    x = qr[:, i, 0:S] if i < 4 else kr[:, 0:S]
                    src = full(dve, ("rope", l, i))
                    do.settle()
                    do(tt(rope_t, src[0:ROPE, 0:S], sinT, ALU.mult), freed(("rope", l, i)))
                    then(tt(x, x, cosT, ALU.mult))
                    do(tt(x, x, rope_t, ALU.add), roped.of((l, i)))
                n = len(tiles[l])
                for i in range(n + 1):
                    if i < n:
                        nk = T if tiles[l][i][0] < 2 else S
                        src = full(dve, ("sc", l, i))
                        do.settle()
                        then(nc.vector.reduce_max(mxt[:, i % 4, 0:1], src[:, 0:nk], AX.X))
                        do(ts(mxt[:, i % 4, 1:2], mxt[:, i % 4, 0:1], -SCALE, None, ALU.mult), row_max.of((l, i)))
                    if i:
                        nk = T if tiles[l][i - 1][0] < 2 else S
                        s = (i - 1) % 4
                        exped.wait(dve, (l, i - 1))
                        then(nc.vector.reciprocal(mxt[:, s, 3:4], mxt[:, s, 2:3]), freed(("sc", l, i - 1)))
                        do(ts(prob[:, s, 0:nk], prob[:, s, 0:nk], mxt[:, s, 3:4], None, ALU.mult), prob_ready.of((l, i - 1)))

            def merge(l):
                W = out_w[l]
                for br in range(3):
                    for d in range(DT):
                        dve.wait_ge(*freed(("gate", l, br, d)))
                        src = full(dve, ("br", l, br, d))
                        g = gate_t[:, (br * DT + d) % 2, 0:W]
                        if br == 0:
                            do(tt(mix[:, d, 0:W], src[:, 0:W], g, ALU.mult), freed(("br", l, br, d)))
                        else:
                            t = part_t[:, d % 2, 0:W]
                            then(tt(t, src[:, 0:W], g, ALU.mult), freed(("br", l, br, d)))
                            do(tt(mix[:, d, 0:W], mix[:, d, 0:W], t, ALU.add), mixed.of((l, d)) if br == 2 else None)
                for d in range(DT):
                    add_to_x(l, 1, ("out", l, d), d, W)

            setup()
            ada_head()
            for l in range(L):
                norm(l, 0)
                ffn(l, 0)
                norm(l, 1)
                mixer_in(l)
                hgrn_out(l)
                hyena(l)
                mla(l)
                merge(l)
                norm(l, 2)
                ffn(l, 1)


def shape_tables():
    f32 = np.float32
    fixed = np.zeros((P, NFIXED), f32)
    fixed[:, 0:128] = np.eye(P)
    inv = (f32(10000.0) ** (-np.arange(0, 32, 2, dtype=f32) / f32(32))).astype(f32)
    row = np.repeat(np.arange(S // 64, dtype=f32), 64)
    col = np.tile(np.arange(64, dtype=f32), S // 64)
    ang = [(v[:, None] * inv).astype(f32).T for v in (row, col)]
    ang = np.concatenate([ang[0], ang[0], ang[1], ang[1]]).astype(np.float64)
    fixed[0:ROPE, 128:384], fixed[0:ROPE, 384:640] = np.cos(ang), np.sin(ang)
    for base in (0, 32):
        for j in range(16):
            fixed[base + 16 + j, 640 + base + j] = -1.0
            fixed[base + j, 640 + base + 16 + j] = 1.0
    t = np.linspace(0.0, 1.0, S, dtype=f32)[:, None]
    w = (f32(2.0 * math.pi / S) * np.arange(S, dtype=f32))[:, None]
    bands = np.linspace(1e-4, 15, 16, dtype=f32)[None, :]
    arg = (bands * w).astype(np.float64)
    fixed[0:EMB, 704:960] = np.concatenate([t, np.cos(arg), -np.sin(arg)], axis=-1).T
    om = 2 * np.pi * (np.arange(S) + 0.5) / 512
    ph = np.arange(S)[:, None] * om[None, :]
    mats = [np.cos(ph), np.sin(ph), np.cos(ph).T, np.sin(ph).T]
    deltas = np.abs(np.linspace(math.log(1e-2) / 1.5, math.log(1e-2) / 0.3, HYW, dtype=f32))
    win = np.exp(-t.astype(np.float64) * deltas) + 0.05
    win_b = win.copy()
    win_b[0] = 0.0
    tab = np.concatenate([m.reshape(2, P, -1).transpose(1, 0, 2).reshape(P, -1) for m in mats + [win, win_b]], 1)
    s, tq = np.arange(P)[:, None], np.arange(P)[None, :]
    masks = np.stack([s == tq] + [(s // (2 * m) == tq // (2 * m)) & (s // m != tq // m) for m in LEVELS[1:]])
    return fixed, tab.astype(f32), np.ascontiguousarray(masks.transpose(1, 0, 2).astype(np.int32))


def lay_out(v):
    def cols(a):
        a = a.reshape(a.shape[:-1] + (-1, P))
        return np.swapaxes(a, -1, -2)

    def chunks(w, width):
        n_l, rows, n = w.shape
        return w.reshape(n_l, rows // P, P, n // width, width).transpose(0, 3, 2, 1, 4)

    out = {}
    out["c"], out["c_ctx"] = v["c"][0], v["c_ctx"]
    x = np.concatenate([v["x"][0], v["ctx"][0]], 0)
    out["xT"] = x.T.reshape(DT, P, T).transpose(1, 0, 2)
    out["ada"] = np.swapaxes(v["ada_w"], 1, 2).reshape(L, MOD_TILES, P, D)
    for f, (a, b) in enumerate((("ffn1_w13", "ffn1_w2"), ("ffn2_w13", "ffn2_w2"))):
        w = v[a].reshape(L, DT, P, 2, FT, P).transpose(0, 4, 2, 3, 1, 5)
        out[f"up{f}"] = w.reshape(L, FT, P, UP_CHUNK)
        out[f"down{f}"] = chunks(v[b], P).reshape(L, DT, P, DOWN_CHUNK)
    w = v["w_in"]
    parts = [w[:, :, 512:1024], w[:, :, 1024:1536], w[:, :, 0:512], w[:, :, 1536:4352]]
    out["proj"] = np.concatenate([chunks(p, 256) for p in parts], 1).reshape(L, 17, P, PROJ_CHUNK)
    out["kvkr"] = chunks(w[:, :, 4352:4544], 192).reshape(L, 1, P, KVKR_CHUNK)
    uq = v["w_uq"].reshape(L, 2, P, 768).transpose(0, 2, 1, 3).reshape(L, P, 1536)
    out["mla"] = np.concatenate([uq, v["w_ukv"]], -1)[:, None]
    merge = []
    for i, name in enumerate(("w_br_a", "w_br_b", "w_br_c")):
        gate = chunks(w[:, :, 4544 + i * D:4544 + (i + 1) * D], 256).reshape(L, 4, P, 2048)
        merge.append(np.concatenate([gate, chunks(v[name], 256).reshape(L, 4, P, 1024)], -1))
    out["merge"] = np.concatenate(merge, 1)
    out["wout"] = chunks(v["w_out"], 256).reshape(L, 4, P, PROJ_CHUNK)
    out["w4"] = v["hy_w4"]
    out["logits"] = v["hg_lb_logits"].reshape(2, L, H, P).transpose(3, 0, 1, 2)
    small = np.zeros((P, L, NSMALL), np.float32)

    def put(name, a):
        at, n = SMALL[name]
        small[0:a.shape[1], :, at:at + n] = np.swapaxes(a, 0, 1)
    for name in ("ffn1_norm", "mix_norm", "ffn2_norm", "ada_b", "hg_out_norm", "q_a_norm", "kv_a_norm",
                 "q_nope_norm", "k_nope_norm"):
        put(name, cols(v[name]))
    put("conv_w", cols(v["hy_conv_w"].reshape(L, -1)))
    put("conv_b", cols(v["hy_conv_b"]))
    put("skip", cols(v["hy_skip"].reshape(L, -1)))
    for name, src in (("b1", "hy_b1"), ("b2", "hy_b2"), ("b3", "hy_b3"), ("freq", "hy_freq"),
                      ("q_rope_norm", "q_rope_norm"), ("k_rope_norm", "k_rope_norm")):
        put(name, v[src][:, :, None])
    for name in ("w1", "w2", "w3"):
        put(name, v["hy_" + name])
    out["small"] = small
    out["fixed"], out["hy_tab"], out["masks"] = shape_tables()
    return {k: np.ascontiguousarray(a) for k, a in out.items()}


def kernel(**inputs):
    import concourse.bacc as bacc
    from concourse.bass_utils import run_bass_kernel_spmd as run

    arrays = lay_out({k: np.asarray(a) for k, a in inputs.items()})
    nc = bacc.Bacc("TRN2", target_bir_lowering=False, num_devices=1)
    dram = {k: nc.dram_tensor(f"in_{k}", a.shape, mybir.dt.from_np(a.dtype), kind="ExternalInput").ap()
            for k, a in arrays.items()}
    out = nc.dram_tensor("out_0", (P, DT, S), mybir.dt.float32, kind="ExternalOutput").ap()
    build(nc, dram, out)
    r = run(nc, [{f"in_{k}": a for k, a in arrays.items()}], core_ids=[0])
    got = r.results[0]["out_0"]
    return np.ascontiguousarray(got.transpose(1, 0, 2).reshape(D, S).T)[None]
```
